# Optimizing a Trainium2 kernel written in Bass

```python
import math
import jax
import jax.numpy as jnp
from jax import lax
import numpy as np

D_MODEL = 1024
BATCH = 1
SEQ = 512
DEPTH = 2

GRID_W = 64
CTX_LEN = 256
N_MIXERS = 2
D_FF = 4 * D_MODEL
NORM_EPS = 1e-6
ROPE_THETA = 10000.0
DN_HEAD_DIM = 128
DN_HEADS = D_MODEL // DN_HEAD_DIM
DN_WIDTH = DN_HEADS * DN_HEAD_DIM
DN_PROJ = 4 * DN_WIDTH + 4 * DN_HEADS
DN_CONV_W = 5
DN_CHUNK = 64
DA_HEAD_DIM = 64
DA_HEADS = D_MODEL // (2 * DA_HEAD_DIM)
DA_V_DIM = 2 * DA_HEAD_DIM
DA_QK_WIDTH = DA_HEADS * 2 * DA_HEAD_DIM
DA_V_WIDTH = DA_HEADS * DA_V_DIM
DA_PROJ = 2 * DA_QK_WIDTH + DA_V_WIDTH
Q_BLOCK = 128
N_DN_LAYERS = (DEPTH + 1) // 2
N_DA_LAYERS = DEPTH // 2

kernel_name = 'hybrid_deltanet_diffattn_dit_block'

def rms_norm(x, w):
    xf = x.astype(jnp.float32)
    y = xf * lax.rsqrt(jnp.mean(xf * xf, axis=-1, keepdims=True) + NORM_EPS)
    return (y * w.astype(jnp.float32)).astype(x.dtype)

def modulate(x, w, shift, scale):
    return rms_norm(x, w) * (1 + scale) + shift

def squared_relu_mlp(h, w1, w2):
    a = jax.nn.relu(h @ w1)
    return (a * a) @ w2

def axial_rope(n_tokens, dim):
    rows = n_tokens // GRID_W
    row = jnp.repeat(jnp.arange(rows, dtype=jnp.int32), GRID_W).astype(jnp.float32)
    col = jnp.tile(jnp.arange(GRID_W, dtype=jnp.int32), rows).astype(jnp.float32)
    n_freq = dim // 4
    inv = ROPE_THETA ** (-jnp.arange(n_freq, dtype=jnp.float32) / n_freq)
    ang = jnp.concatenate([row[:, None] * inv, col[:, None] * inv], axis=-1)
    return jnp.cos(ang), jnp.sin(ang)

def apply_rope(x, cos, sin):
    half = x.shape[-1] // 2
    x1, x2 = x[..., :half], x[..., half:]
    cos = cos[:, None, None, :].astype(x.dtype)
    sin = sin[:, None, None, :].astype(x.dtype)
    return jnp.concatenate([x1 * cos - x2 * sin, x1 * sin + x2 * cos], axis=-1)

def short_conv(x, w):
    pad = (DN_CONV_W - 1) // 2
    y = lax.conv_general_dilated(x, w[:, None, :].astype(x.dtype), window_strides=(1,),
                                 padding=[(pad, pad)], dimension_numbers=('NWC', 'WIO', 'NWC'),
                                 feature_group_count=x.shape[-1])
    return jax.nn.silu(y)

def l2_normalize(x):
    xf = x.astype(jnp.float32)
    return xf * lax.rsqrt(jnp.sum(xf * xf, axis=-1, keepdims=True) + 1e-6)

def gated_delta_chunked(q, k, v, g, beta, s0):
    b, h, t, dk = q.shape
    dv = v.shape[-1]
    n = t // DN_CHUNK
    q = q.reshape(b, h, n, DN_CHUNK, dk)
    k = k.reshape(b, h, n, DN_CHUNK, dk)
    v = v.reshape(b, h, n, DN_CHUNK, dv)
    g = g.reshape(b, h, n, DN_CHUNK)
    beta = beta.reshape(b, h, n, DN_CHUNK)
    G = jnp.cumsum(g, axis=-1)
    idx = jnp.arange(DN_CHUNK)
    incl = idx[:, None] >= idx[None, :]
    strict = idx[:, None] > idx[None, :]
    decay = jnp.exp(jnp.where(incl, G[..., :, None] - G[..., None, :], -jnp.inf))
    kk = jnp.einsum('bhnid,bhnjd->bhnij', k, k)
    a_mat = jnp.where(strict, kk * decay * beta[..., :, None], 0.0)
    unit_lower = a_mat + jnp.eye(DN_CHUNK, dtype=q.dtype)
    rhs = jnp.concatenate([v * beta[..., None], k * (beta * jnp.exp(G))[..., None]], axis=-1)
    sol = lax.linalg.triangular_solve(unit_lower, rhs, left_side=True, lower=True, unit_diagonal=True)
    u, w = sol[..., :dv], sol[..., dv:]
    qk = jnp.einsum('bhnid,bhnjd->bhnij', q, k) * decay
    q_dec = q * jnp.exp(G)[..., None]
    k_dec = k * jnp.exp(G[..., -1:] - G)[..., None]
    g_tot = jnp.exp(G[..., -1])

    def step(state, xs):
        u_c, w_c, qk_c, qd_c, kd_c, gt_c = xs
        nu = u_c - jnp.einsum('bhcd,bhde->bhce', w_c, state)
        out = jnp.einsum('bhcd,bhde->bhce', qd_c, state) + jnp.einsum('bhij,bhje->bhie', qk_c, nu)
        state = state * gt_c[..., None, None] + jnp.einsum('bhcd,bhce->bhde', kd_c, nu)
        return state, out

    xs = (jnp.moveaxis(u, 2, 0), jnp.moveaxis(w, 2, 0), jnp.moveaxis(qk, 2, 0),
          jnp.moveaxis(q_dec, 2, 0), jnp.moveaxis(k_dec, 2, 0), jnp.moveaxis(g_tot, 2, 0))
    s_final, o = lax.scan(step, s0, xs)
    o = jnp.moveaxis(o, 0, 2).reshape(b, h, t, dv)
    return o, s_final

def deltanet_mixer(h_lat, h_ctx, w_in, conv_w, a_log, dt_bias, out_norm, w_out, with_ctx_out):
    def prep(hs):
        bsz, t, _ = hs.shape
        proj = hs @ w_in
        qkv = short_conv(proj[..., :3 * DN_WIDTH], conv_w)
        z = proj[..., 3 * DN_WIDTH:4 * DN_WIDTH]
        gate_in = proj[..., 4 * DN_WIDTH:].astype(jnp.float32)

        def heads(y):
            return y.reshape(bsz, t, DN_HEADS, DN_HEAD_DIM).transpose(0, 2, 1, 3)

        q = l2_normalize(heads(qkv[..., :DN_WIDTH])) * (DN_HEAD_DIM ** -0.5)
        k = l2_normalize(heads(qkv[..., DN_WIDTH:2 * DN_WIDTH]))
        v = heads(qkv[..., 2 * DN_WIDTH:]).astype(jnp.float32)
        a_dir = gate_in[..., :2 * DN_HEADS].reshape(bsz, t, 2, DN_HEADS)
        b_dir = gate_in[..., 2 * DN_HEADS:].reshape(bsz, t, 2, DN_HEADS)
        g = -jnp.exp(a_log.astype(jnp.float32)) * jax.nn.softplus(a_dir + dt_bias.astype(jnp.float32))
        beta = jax.nn.sigmoid(b_dir)
        return q, k, v, g.transpose(2, 0, 3, 1), beta.transpose(2, 0, 3, 1), z

    qc, kc, vc, gc, bc, zc = prep(h_ctx)
    ql, kl, vl, gl, bl, zl = prep(h_lat)
    s0 = jnp.zeros((h_lat.shape[0], DN_HEADS, DN_HEAD_DIM, DN_HEAD_DIM), jnp.float32)

    def flip(y):
        return jnp.flip(y, axis=2)

    oc_f, sc_f = gated_delta_chunked(qc, kc, vc, gc[0], bc[0], s0)
    ol_f, _ = gated_delta_chunked(ql, kl, vl, gl[0], bl[0], sc_f)
    oc_b, sc_b = gated_delta_chunked(flip(qc), flip(kc), flip(vc), flip(gc[1]), flip(bc[1]), s0)
    ol_b, _ = gated_delta_chunked(flip(ql), flip(kl), flip(vl), flip(gl[1]), flip(bl[1]), sc_b)

    def finish(o, z):
        bsz, t = z.shape[:2]
        o = o.transpose(0, 2, 1, 3).astype(z.dtype)
        y = rms_norm(o, out_norm) * jax.nn.silu(z.reshape(bsz, t, DN_HEADS, DN_HEAD_DIM))
        return y.reshape(bsz, t, DN_WIDTH) @ w_out

    y_lat = finish(ol_f + flip(ol_b), zl)
    y_ctx = finish(oc_f + flip(oc_b), zc) if with_ctx_out else None
    return y_lat, y_ctx

def diff_attn_mixer(h_lat, h_ctx, w_qkv, lam, subln, w_out, lambda_init, with_ctx_out):
    def prep(hs):
        bsz, t, _ = hs.shape
        proj = hs @ w_qkv
        q = proj[..., :DA_QK_WIDTH].reshape(bsz, t, DA_HEADS, 2, DA_HEAD_DIM) * (DA_HEAD_DIM ** -0.5)
        k = proj[..., DA_QK_WIDTH:2 * DA_QK_WIDTH].reshape(bsz, t, DA_HEADS, 2, DA_HEAD_DIM)
        v = proj[..., 2 * DA_QK_WIDTH:].reshape(bsz, t, DA_HEADS, DA_V_DIM)
        return q, k, v

    lamf = lam.astype(jnp.float32)
    lambda_full = jnp.exp(jnp.sum(lamf[0] * lamf[1])) - jnp.exp(jnp.sum(lamf[2] * lamf[3])) + lambda_init

    def attend(qb, keys, vals):
        s = jnp.einsum('bqhmd,bkhmd->bhmqk', qb, keys).astype(jnp.float32)
        p = jax.nn.softmax(s, axis=-1)
        p = (p[:, :, 0] - lambda_full * p[:, :, 1]).astype(vals.dtype)
        return jnp.einsum('bhqk,bkhe->bqhe', p, vals)

    def finish(o):
        bsz, t = o.shape[:2]
        y = rms_norm(o, subln) * (1.0 - lambda_init)
        return y.reshape(bsz, t, DA_V_WIDTH) @ w_out

    qc, kc, vc = prep(h_ctx)
    ql, kl, vl = prep(h_lat)
    bsz, t_lat = h_lat.shape[:2]
    cos, sin = axial_rope(t_lat, DA_HEAD_DIM)
    ql = apply_rope(ql, cos, sin)
    kl = apply_rope(kl, cos, sin)
    k_all = jnp.concatenate([kc, kl], axis=1)
    v_all = jnp.concatenate([vc, vl], axis=1)
    n_blocks = t_lat // Q_BLOCK
    q_blocks = ql.reshape(bsz, n_blocks, Q_BLOCK, DA_HEADS, 2, DA_HEAD_DIM).transpose(1, 0, 2, 3, 4, 5)
    ol = lax.map(lambda qb: attend(qb, k_all, v_all), q_blocks)
    ol = ol.transpose(1, 0, 2, 3, 4).reshape(bsz, t_lat, DA_HEADS, DA_V_DIM)
    y_lat = finish(ol)
    y_ctx = finish(attend(qc, kc, vc)) if with_ctx_out else None
    return y_lat, y_ctx

def setup_inputs(seed: int = 0) -> dict:
    key = jax.random.key(seed)
    ks = jax.random.split(key, 20)
    f32 = jnp.float32

    def normal(k, shape, scale):
        return jax.random.normal(k, shape, f32) * scale

    dt = jnp.exp(jax.random.uniform(ks[12], (N_DN_LAYERS, 2, DN_HEADS), f32,
                                    math.log(1e-3), math.log(1e-1)))
    return {
        'x': normal(ks[0], (BATCH, SEQ, D_MODEL), 1.0),
        'c': normal(ks[1], (BATCH, D_MODEL), 1.0),
        'ctx': normal(ks[2], (BATCH, CTX_LEN, D_MODEL), 1.0),
        'c_ctx': normal(ks[3], (D_MODEL,), 1.0),
        'ada_w': normal(ks[4], (DEPTH, D_MODEL, 6 * D_MODEL), 0.5 * D_MODEL ** -0.5),
        'ada_b': normal(ks[5], (DEPTH, 6 * D_MODEL), 0.02),
        'norm_w': 1.0 + normal(ks[6], (DEPTH, 2, D_MODEL), 0.02),
        'mlp_w1': normal(ks[7], (DEPTH, D_MODEL, D_FF), D_MODEL ** -0.5),
        'mlp_w2': normal(ks[8], (DEPTH, D_FF, D_MODEL), D_FF ** -0.5),
        'dn_w_in': normal(ks[9], (N_DN_LAYERS, D_MODEL, DN_PROJ), D_MODEL ** -0.5),
        'dn_conv': normal(ks[10], (N_DN_LAYERS, DN_CONV_W, 3 * DN_WIDTH), DN_CONV_W ** -0.5),
        'dn_a_log': jnp.log(jax.random.uniform(ks[11], (N_DN_LAYERS, 2, DN_HEADS), f32, 1.0, 16.0)),
        'dn_dt_bias': dt + jnp.log(-jnp.expm1(-dt)),
        'dn_out_norm': 1.0 + normal(ks[13], (N_DN_LAYERS, DN_HEAD_DIM), 0.02),
        'dn_w_out': normal(ks[14], (N_DN_LAYERS, DN_WIDTH, D_MODEL), DN_WIDTH ** -0.5),
        'da_w_qkv': normal(ks[15], (N_DA_LAYERS, D_MODEL, DA_PROJ), D_MODEL ** -0.5),
        'da_lambda': normal(ks[16], (N_DA_LAYERS, 4, DA_HEAD_DIM), 0.1),
        'da_subln': 1.0 + normal(ks[17], (N_DA_LAYERS, DA_V_DIM), 0.02),
        'da_w_out': normal(ks[18], (N_DA_LAYERS, DA_V_WIDTH, D_MODEL), DA_V_WIDTH ** -0.5),
        'final_norm': 1.0 + normal(ks[19], (D_MODEL,), 0.02),
    }

def reference(x, c, ctx, c_ctx, ada_w, ada_b, norm_w, mlp_w1, mlp_w2, dn_w_in, dn_conv, dn_a_log,
              dn_dt_bias, dn_out_norm, dn_w_out, da_w_qkv, da_lambda, da_subln, da_w_out, final_norm):
    xc = ctx
    silu_c = jax.nn.silu(c)
    silu_cc = jax.nn.silu(c_ctx)
    for i in range(DEPTH):
        last = i == DEPTH - 1
        m_lat = jnp.split((silu_c @ ada_w[i] + ada_b[i])[:, None, :], 6, axis=-1)
        m_ctx = jnp.split(silu_cc @ ada_w[i] + ada_b[i], 6, axis=-1)
        h_lat = modulate(x, norm_w[i, 0], m_lat[0], m_lat[1])
        h_ctx = modulate(xc, norm_w[i, 0], m_ctx[0], m_ctx[1])
        j = i // N_MIXERS
        if i % N_MIXERS == 0:
            y_lat, y_ctx = deltanet_mixer(h_lat, h_ctx, dn_w_in[j], dn_conv[j], dn_a_log[j], dn_dt_bias[j],
                                          dn_out_norm[j], dn_w_out[j], not last)
        else:
            lambda_init = 0.8 - 0.6 * math.exp(-0.3 * i)
            y_lat, y_ctx = diff_attn_mixer(h_lat, h_ctx, da_w_qkv[j], da_lambda[j], da_subln[j], da_w_out[j],
                                           lambda_init, not last)
        x = x + m_lat[2] * y_lat
        x = x + m_lat[5] * squared_relu_mlp(modulate(x, norm_w[i, 1], m_lat[3], m_lat[4]), mlp_w1[i], mlp_w2[i])
        if not last:
            xc = xc + m_ctx[2] * y_ctx
            xc = xc + m_ctx[5] * squared_relu_mlp(modulate(xc, norm_w[i, 1], m_ctx[3], m_ctx[4]),
                                                  mlp_w1[i], mlp_w2[i])
    return rms_norm(x, final_norm)


_drawn_inputs = setup_inputs


def setup_inputs(seed=0):
    import zlib

    import numpy as np

    out = dict(_drawn_inputs(seed))
    spreads = {}
    factors = {'norm_w': 3.962,
     'dn_out_norm': 8.0,
     'da_lambda': 4.396,
     'da_subln': 8.0,
     'final_norm': 2.842}
    for name, (base, spread) in spreads.items():
        noise = np.random.default_rng([zlib.crc32(name.encode()), seed]).standard_normal(out[name].shape)
        drawn = base * np.exp(spread * noise) if base else spread * noise
        out[name] = jnp.asarray(drawn.astype(out[name].dtype))
    for name, factor in factors.items():
        out[name] = (out[name] * factor).astype(out[name].dtype)
    return out
```

```python
from contextlib import ExitStack

import numpy as np

import concourse.bass as bass
from concourse import mybir

F32 = mybir.dt.float32
F32R = mybir.dt.float32r
ACT = mybir.ActivationFunctionType
ALU = mybir.AluOpType
AX_X = mybir.AxisListType.X

P = 128
D = 1024
KC = D // P
CTX, LAT = 256, 512
TOK = CTX + LAT
NT = TOK // P
HEADS = 8
SLOT = TOK + 4
EPS = 1e-6
LAMBDA_INIT = float(0.8 - 0.6 * np.exp(-0.3))
LEVELS = 7
NM = 2 * NT
LATS, CTXS = slice(CTX, TOK), slice(0, CTX)
GROUPS = ((LATS, LAT, 0), (CTXS, CTX, 1))
S_DNIN, S_DNOUT, S_MLP0, S_QKV, S_DAOUT, S_MLP1, S_END = 0, 32, 40, 104, 128, 136, 200
ORDER = (tuple(range(NT)), (1, 0, 5, 4, 3, 2))


def off(c):
    return P * c + (4 if c >= 2 else 0)


def constants():
    p, f = np.indices((P, P))
    tri = [p == f, p >= 0, p <= f, p >= f, p > f, p < f]
    masks = []
    for d in range(2):
        for level in range(LEVELS):
            s = 1 << level
            m = (p // (2 * s) == f // (2 * s)) & ((p // s) % 2 == 0) & ((f // s) % 2 == 1)
            masks.append(m if d == 0 else m.T)
    cst = np.concatenate([x.astype(np.float32) for x in tri], axis=1)
    lvl = np.concatenate([x.astype(np.float32) for x in masks], axis=1)
    n = np.arange(LAT)
    inv = np.float32(10000.0) ** (-np.arange(16, dtype=np.float32) / np.float32(16))
    row, col = (n // 64).astype(np.float32), (n % 64).astype(np.float32)
    ang = np.concatenate([row[:, None] * inv, col[:, None] * inv], axis=1)
    cos, sin = np.cos(ang).T, np.sin(ang).T
    rope = np.concatenate([np.tile(cos, (4, 1)), np.concatenate([-sin, sin, -sin, sin])], axis=1)
    return cst, lvl, rope.astype(np.float32)


def build(nc, A):
    ctx = ExitStack()
    with ctx:
        top = [16512]
        nc_off = {}

        def at(name, shape, dt=F32, where=None):
            size = int(np.prod(shape[1:])) * 4
            if where is None:
                where = top[0]
                top[0] += (size + 31) // 32 * 32
            nc_off[name] = where
            t = nc.alloc_sbuf_tensor_at(name, shape, dt, offset=where)
            return t

        def sem(name):
            return ctx.enter_context(nc.semaphore(name))

        cst = at("cst", [P, 6, P])
        ident, ones = cst[:, 0, :], cst[:, 1, :]
        CUM = (cst[:, 2, :], cst[:, 3, :])
        STRICT = (cst[:, 4, :], cst[:, 5, :])
        xT = at("xT", [P, KC, TOK])
        raw = [at(f"raw{i}", [P, KC, 2 * P]) for i in range(2)]
        whi = [at(f"whi{i}", [P, KC, P], F32R) for i in range(2)]
        wlo = [at(f"wlo{i}", [P, KC, P], F32R) for i in range(2)]
        vecT = at("vecT", [P, 3, P])
        mods = at("mods", [P, 2, 48, 2])
        wmod = at("wmod", [P, 4, KC, 2])
        allsc = at("allsc", [P, 5, NT, 16])
        gates = at("gates", [P, NT, 32])
        gtmp = at("gtmp", [P, 4, NT, 16])
        gdec = at("gdec", [P, NT, 16])
        sc32 = at("sc32", [P, 4, 16])
        cT = at("cT", [P, KC, 2])
        eps, one = at("eps", [P, 1]), at("one", [P, 1])
        region_h = top[0]
        hh = at("hh", [P, KC, TOK], F32R)
        hl = at("hl", [P, KC, TOK], F32R)
        region_s = top[0]
        rstd = at("rstd", [P, TOK])
        xn = at("xn", [P, 2, TOK])
        hm = at("hm", [P, TOK])
        top[0] = region_s + 12416
        adaw = [at(f"adaw{i}", [P, KC, P]) for i in range(2)]
        region_q = top[0]
        qkv = at("qkv", [P, 24, SLOT])
        assert top[0] <= 229344, top[0]
        xr = at("xr", [P, 2, SLOT + 4], where=region_s)
        cv = at("cv", [P, 2, SLOT], where=region_s + 6208)
        zst = at("zst", [P, 2, TOK], where=region_s)
        xin = at("xin", [P, NT, D], where=region_q)
        sqb = at("sqb", [P, KC, TOK], where=region_q + 24576)
        vecR = at("vecR", [P, 3, P], where=region_q + 49152)
        wgr = at("wgr", [P, KC, 32], where=region_q + 64000)
        wgh = at("wgh", [P, KC, 32], F32R, where=region_q + 65024)
        wgl = at("wgl", [P, KC, 32], F32R, where=region_q + 66048)
        top[0] = region_h
        lvl = at("lvl", [P, 2, LEVELS, P])
        Am = at("Am", [P, NM, P])
        TU = at("TU", [P, 2, NM, P])
        Pm = at("Pm", [P, NM, P])
        QKT = at("QKT", [P, NM, P])
        qd = at("qd", [P, NM, P])
        kN = at("kN", [P, NT, P])
        vN = at("vN", [P, NT, P])
        qS = at("qS", [P, SLOT])
        kS = at("kS", [P, SLOT])
        vS = at("vS", [P, SLOT])
        SC = at("SC", [P, 5, 2, NT])
        St = [at(f"S{d}", [P, P]) for d in range(2)]
        rr = [at(f"rr{d}", [P, P]) for d in range(2)]
        nu = [at(f"nu{d}", [P, P]) for d in range(2)]
        nuk = [at(f"nuk{d}", [P, P]) for d in range(2)]
        assert top[0] <= region_q, (top[0], region_q)
        OB = vS
        l2b = at("l2b", [P, 2, SLOT], where=nc_off["QKT"])
        zin = at("zin", [P, HEADS, TOK], where=region_q + 16 * 4 * SLOT)
        hidh = at("hidh", [P, KC, TOK], F32R, where=region_q)
        hidl = at("hidl", [P, KC, TOK], F32R, where=region_q + 24576)
        mtmp = at("mtmp", [P, 2, TOK], where=region_q + 49152)
        msq = at("msq", [P, 2, TOK], where=region_q + 55296)
        qT = at("qT", [P, HEADS, LAT], where=region_q)
        kT = at("kT", [P, HEADS, TOK], where=region_q + 16384)
        vT = at("vT", [P, HEADS, TOK], where=region_q + 40960)
        ropt = at("ropt", [P, 2, LAT], where=region_s)
        rsw = at("rsw", [P, 2, LAT], where=region_s + 4096)
        rcs = at("rcs", [P, LAT], where=region_s + 8192)
        lamb = at("lamb", [P, 2, 2, 64], where=region_s + 10240)
        atop = region_h
        qz = at("qz", [P, 2, LAT], where=atop)
        vn = at("vn", [P, NT, P], where=atop + 4096)
        pr = at("pr", [P, 2, 2, TOK], where=atop + 7168)
        pc = at("pc", [P, 2, TOK], where=atop + 19456)
        pT = at("pT", [P, NT, LAT], where=atop + 25600)
        ast = at("ast", [P, 8, 8], where=atop + 37888)
        vs2 = at("vs2", [P, TOK], where=atop + 38400)
        osq = at("osq", [P, 2, LAT], where=atop + 41472)
        orr = at("orr", [P, LAT], where=atop + 45568)
        fin = at("fin", [P, 4, D], where=region_q + 49152)

        bank = ctx.enter_context(nc.psum_tensor("bank", [P, 8, 512], F32))
        pb = [bank[:, i, :] for i in range(8)]
        sps = [bank[:, 2 + 2 * m:4 + 2 * m, :] for m in range(2)]
        zdram = nc.dram_tensor("z_scratch", [HEADS, P, TOK], F32, kind="Internal").ap()

        s_cst, s_x, s_vec, s_wg = sem("s_cst"), sem("s_x"), sem("s_vec"), sem("s_wg")
        s_raw = [sem(f"s_raw{i}") for i in range(2)]
        s_ada = [sem(f"s_ada{i}") for i in range(2)]
        hi_done, lo_done, proj_done, drained = sem("hi_done"), sem("lo_done"), sem("proj_done"), sem("drained")
        ada_done, adaw_used = sem("ada_done"), sem("adaw_used")
        xin_t, xT_ready = sem("xin_t"), sem("xT_ready")
        vec_t, vec_ready, c_ready = sem("vec_t"), sem("vec_ready"), sem("c_ready")
        mod_ready = sem("mod_ready")
        sq_ready, ss_ready, sd_ready, rs_ready = sem("sq_ready"), sem("ss_ready"), sem("sd_ready"), sem("rs_ready")
        xn_ready, hm_ready, hh_ready, hl_ready = sem("xn_ready"), sem("hm_ready"), sem("hh_ready"), sem("hl_ready")
        pads, wg_hi, wg_lo, gate_ps, gate_raw = sem("pads"), sem("wg_hi"), sem("wg_lo"), sem("gate_ps"), sem("gate_raw")
        kon, a_mods = sem("kon"), sem("a_mods")
        sc_all, xT_lat, xT_ctx = sem("sc_all"), sem("xT_lat"), sem("xT_ctx")
        o_sum = [sem(f"o_sum{d}") for d in range(2)]
        ga, gv, gp = sem("ga"), sem("gv"), sem("gp")
        xr_ready, conv_step, silu_done, z_ready, zs = sem("xr_ready"), sem("conv_step"), sem("silu_done"), sem("z_ready"), [sem(f"z_stored{i}") for i in range(2)]
        x_res = sem("x_res")
        relu_done, sq_done, hid_hi, hid_lo = sem("relu_done"), sem("sq_done"), sem("hid_hi"), sem("hid_lo")
        s_lvl, s_zin = sem("s_lvl"), sem("s_zin")
        l2_sq, l2_ss, l2_sd, l2_rc, qk_ready = sem("l2_sq"), sem("l2_ss"), sem("l2_sd"), sem("l2_rc"), sem("qk_ready")
        sc_ready, gu_ready, grow_ps, eg_ready = sem("sc_ready"), sem("gu_ready"), sem("grow_ps"), sem("eg_ready")
        x_ready, xm_ready, dec_ready, qd_ready = sem("x_ready"), sem("xm_ready"), sem("dec_ready"), sem("qd_ready")
        vs_ready, kv_t, kv_nat, kk_ps, qk_ps = sem("vs_ready"), sem("kv_t"), sem("kv_nat"), sem("kk_ps"), sem("qk_ps")
        am_step, qkt_step, tu_init = sem("am_step"), sem("qkt_step"), sem("tu_init")
        p_ps, p_ready, x_ps, tu_ready, ub_ready = sem("p_ps"), sem("p_ready"), sem("x_ps"), sem("tu_ready"), sem("ub_ready")
        s_init = sem("s_init")
        ks_ps = [sem(f"ks_ps{d}") for d in range(2)]
        r_ready = [sem(f"r_ready{d}") for d in range(2)]
        nu_ps = [sem(f"nu_ps{d}") for d in range(2)]
        nu_ready = [sem(f"nu_ready{d}") for d in range(2)]
        o_ps = [sem(f"o_ps{d}") for d in range(2)]
        ds_ps = [sem(f"ds_ps{d}") for d in range(2)]
        s_new = [sem(f"s_new{d}") for d in range(2)]
        head_out = sem("head_out")
        f_sq, f_ss, f_sd, f_rc, f_y1, f_y = sem("f_sq"), sem("f_ss"), sem("f_sd"), sem("f_rc"), sem("f_y1"), sem("f_y")
        y_hi, y_lo = sem("y_hi"), sem("y_lo")
        s_rope, rp_sw, rp_cos, rp_sin, k_ready, v_ready = sem("s_rope"), sem("rp_sw"), sem("rp_cos"), sem("rp_sin"), sem("k_ready"), sem("v_ready")
        lam_a, lam_v, lam_p = sem("lam_a"), sem("lam_v"), sem("lam_p")
        qz_zero, qz_ready, vt_ps, vn_ready = sem("qz_zero"), sem("qz_ready"), sem("vt_ps"), sem("vn_ready")
        s_ps, mx_ready, nm_ready, e_ready, rl_ready = sem("s_ps"), sem("mx_ready"), sem("nm_ready"), sem("e_ready"), sem("rl_ready")
        p0_ready, pc_ready, pt_ps, pT_ready, at_ps = sem("p0_ready"), sem("pc_ready"), sem("pt_ps"), sem("pT_ready"), sem("at_ps")
        a_sq, a_ss, a_sd, a_rc, a_y = sem("a_sq"), sem("a_ss"), sem("a_sd"), sem("a_rc"), sem("a_y")
        fin_n, fin_ps, fin_ready, s_out = sem("fin_n"), sem("fin_ps"), sem("fin_ready"), sem("s_out")

        block = ctx.enter_context(nc.Block())

        def ds(i, n=1):
            return slice(i, i + n) if isinstance(i, int) else bass.ds(i, n)

        def row(t, i):
            return t[:, ds(i), :].rearrange("p a n -> p (a n)")

        def bc(ap, n):
            return ap.unsqueeze(2).broadcast_to([P, ap.shape[1], n])

        def over(ap, n):
            return ap.unsqueeze(1).broadcast_to([P, n, ap.shape[1]])

        def chunks(t, c0, n):
            return t[:, off(c0):off(c0) + n * P].rearrange("p (c i) -> p c i", i=P)

        def kview(w):
            return w.rearrange("(k p) n -> p k n", p=P)

        def tu_ap(g, level):
            s, d = 1 << level, g // 2
            par_t, par_u = (0, 1) if d == 0 else (1, 0)
            return bass.AP(TU[:, 0, 0, :].tensor, 3 * g * P + par_t * s,
                           [[2 * NM * P, P], [NM * P + (par_u - par_t) * s, 2], [2 * s, 3 * P // (2 * s)], [1, s]])

        def half(ap, s, par):
            return ap.rearrange("p (b two c) -> p b two c", two=2, c=s)[:, :, par, :]

        norm_tokens = {0: GROUPS, 1: GROUPS, 2: GROUPS, 3: GROUPS[:1], 4: GROUPS[:1]}

        def gate(layer, part, o, v):
            return mods[:, layer, part * KC + o, v:v + 1]

        @block.sync
        def _(sp):
            sp.dma_start(cst[:, :, :], A["cst"].rearrange("p (a n) -> p a n", a=6)).then_inc(s_cst, 16)
            sp.dma_start(vecR[0:48, 0, :], A["ada_b"][0].rearrange("(r n) -> r n", n=P)).then_inc(s_vec, 16)
            sp.dma_start(vecR[48:96, 0, :], A["ada_b"][1].rearrange("(r n) -> r n", n=P)).then_inc(s_vec, 16)
            sp.dma_start(vecR[96:128, 0, :], A["norm_w"].rearrange("i j (r n) -> (i j r) n", n=P)).then_inc(s_vec, 16)
            sp.dma_start(vecR[0:120, 1, :], A["dn_conv"][0].rearrange("w (r n) -> (w r) n", n=P)).then_inc(s_vec, 16)
            sp.dma_start(vecR[120:128, 1, :], A["final_norm"].rearrange("(r n) -> r n", n=P)).then_inc(s_vec, 16)
            sp.dma_start(vecR[0:8, 2, :], A["c"][0].rearrange("(r n) -> r n", n=P)).then_inc(s_vec, 16)
            sp.dma_start(vecR[8:16, 2, :], A["c_ctx"].rearrange("(r n) -> r n", n=P)).then_inc(s_vec, 16)
            sp.dma_start(vecR[16:17, 2, :], A["dn_out_norm"]).then_inc(s_vec, 16)
            sp.dma_start(vecR[17:18, 2, :], A["da_subln"]).then_inc(s_vec, 16)
            sp.dma_start(xin[:, 0:2, :], A["ctx"][0].rearrange("(t p) d -> p t d", p=P)).then_inc(s_x, 16)
            sp.dma_start(xin[:, 2:6, :], A["x"][0].rearrange("(t p) d -> p t d", p=P)).then_inc(s_x, 16)

            def load_ada(layer, a, slot, tile, free=None):
                if free is not None:
                    sp.wait_ge(ada_done, free)
                sp.dma_start(adaw[slot][:, :, :], kview(A["ada_w"][layer])[:, :, ds(tile * P, P)]).then_inc(s_ada[slot], 16)

            def load_w(g, slot, src, first=False):
                if not first:
                    sp.wait_ge(lo_done, 2 * g - 2)
                sp.dma_start(raw[slot][:, :, :], src).then_inc(s_raw[slot], 16)

            w_in = kview(A["dn_w_in"][0])
            load_ada(0, 0, 0, 0)
            load_ada(0, 1, 1, 1)
            sp.dma_start(wgr[:, :, :], w_in[:, :, 4096:4128]).then_inc(s_wg, 16)
            sp.dma_start(sc32[:, 0, :], A["dn_a_log"].rearrange("a d h -> a (d h)").broadcast_to([P, 16])).then_inc(s_wg, 16)
            sp.dma_start(sc32[:, 1, :], A["dn_dt_bias"].rearrange("a d h -> a (d h)").broadcast_to([P, 16])).then_inc(s_wg, 16)
            for j in range(2):
                load_w(j, j, w_in[:, :, 256 * j:256 * (j + 1)], first=True)
            with sp.Fori(1, 8) as i:
                for j in range(2):
                    load_ada(0, 2 * i + j, j, 2 * i + j, free=2 * i + j - 1)

            def dnin_loads(b, skip=False):
                for j in range(2):
                    if not skip:
                        load_w(2 * b + j, j, w_in[:, :, ds((2 * b + j) * 256, 256)])
                    for v in range(2):
                        tile = 16 + 4 * b + 2 * j + v
                        load_ada(0, tile, v, tile, free=tile - 1)

            dnin_loads(0, skip=True)
            with sp.Fori(1, 8) as b:
                dnin_loads(b)
            sp.wait_ge(proj_done, S_DNOUT)
            sp.dma_start(lvl[:, :, :, :], A["lvl"].rearrange("p (d l n) -> p d l n", d=2, l=LEVELS)).then_inc(s_lvl, 16)
            w_out = kview(A["dn_w_out"][0])
            g0 = S_DNOUT // 2
            for j in range(4):
                load_w(g0 + j, j % 2, w_out[:, :, 256 * j:256 * (j + 1)])
                if j == 1:
                    sp.wait_ge(head_out, HEADS)
                    sp.dma_start(zin[:, :, :], zdram.rearrange("h p n -> p h n")).then_inc(s_zin, 16)

            def mlp_loads(layer, blk, g0):
                w1, w2 = kview(A["mlp_w1"][layer]), kview(A["mlp_w2"][layer])
                for j in range(8):
                    if j < 4:
                        src = w1[:, :, ds(blk * 1024 + 256 * j, 256)]
                    else:
                        src = w2[:, ds(blk * 8, 8), 256 * (j - 4):256 * (j - 3)]
                    load_w(g0 + 8 * blk + j, j % 2, src)
                    if layer == 0 and j < 6:
                        for v in range(2):
                            tile = 12 * blk + 2 * j + v
                            load_ada(1, tile, v, tile, free=48 + tile - 1)

            with sp.Fori(0, 4) as blk:
                mlp_loads(0, blk, S_MLP0 // 2)
            w_qkv, g0 = kview(A["da_w_qkv"][0]), S_QKV // 2

            def qkv_loads(b):
                for j in range(2):
                    load_w(g0 + 2 * b + j, j, w_qkv[:, :, ds((2 * b + j) * 256, 256)])

            qkv_loads(0)
            sp.wait_ge(hl_ready, 24)
            sp.dma_start(ropt[:, :, :], A["rope"].rearrange("p (a n) -> p a n", a=2)).then_inc(s_rope, 16)
            sp.dma_start(lamb[:, :, :, :].rearrange("p a b n -> p (a b n)"),
                         A["da_lambda"].rearrange("a r n -> a (r n)").broadcast_to([P, 256])).then_inc(s_rope, 16)
            with sp.Fori(1, 6) as b:
                qkv_loads(b)
            w_out2, g0 = kview(A["da_w_out"][0]), S_DAOUT // 2
            for j in range(4):
                load_w(g0 + j, j % 2, w_out2[:, :, 256 * j:256 * (j + 1)])
            with sp.Fori(0, 4) as blk:
                mlp_loads(1, blk, S_MLP1 // 2)
            for t in range(4):
                sp.wait_ge(fin_ready, 2 * t + 2)
                sp.dma_start(A["out"][0, t * P:(t + 1) * P, :], fin[:, t, :]).then_inc(s_out, 16)
            sp.wait_ge(s_out, 64)

        @block.gpsimd
        def _(pool):
            pool.memset(eps[:, :], EPS)
            pool.memset(one[:, :], 1.0).then_inc(kon, 1)
            pool.wait_ge(hl_ready, 8)
            for t in range(2):
                pool.memset(xr[:, t, 0:2], 0.0)
                pool.memset(xr[:, t, 258:262], 0.0)
                pool.memset(xr[:, t, 774:776], 0.0).then_inc(pads, 1)
            for h in range(HEADS):
                pool.wait_ge(drained, 24 + h + 1)
                pool.dma_start(zdram[h], zst[:, h % 2, :]).then_inc(zs[h % 2], 16)
            pool.wait_ge(zs[0], 64)
            pool.wait_ge(zs[1], 64)

            def head_prep(n, first=False):
                if first:
                    pool.wait_ge(silu_done, 24)
                    pool.wait_ge(sc_all, 1)
                    pool.wait_ge(proj_done, S_DNOUT)
                else:
                    pool.wait_ge(head_out, n)
                pool.tensor_copy(vS[:, 0:SLOT], row(qkv, 16 + n)).then_inc(vs_ready, 1)
                for k in range(5):
                    i = pool.tensor_copy(SC[:, k, :, :],
                                         allsc[:, k, :, :].rearrange("p c (d h) -> p d c h", d=2)[:, :, :, ds(n)].rearrange("p d c h -> p d (c h)"))
                i.then_inc(sc_ready, 1)
                for d in range(2):
                    g = gdec[:, :, ds(n + 8 * d)].rearrange("p c h -> p (c h)")
                    pool.tensor_tensor(Pm[:, d * NT:(d + 1) * NT, :], over(CUM[d], NT), bc(g, P), ALU.mult).then_inc(gu_ready, 1)
                pool.tensor_copy(TU[:, 0, :, :], over(ident, NM))
                pool.tensor_copy(TU[:, 1, :, :], over(ident, NM)).then_inc(tu_init, 1)

            head_prep(0, first=True)
            with pool.Fori(1, HEADS) as n:
                head_prep(n)

        @block.scalar
        def _(act):
            def split(s, slot, par, nth):
                act.wait_ge(s_raw[slot], nth)
                if not isinstance(s, int) or s >= 2:
                    act.wait_ge(proj_done, s - 1)
                act.activation(whi[par][:, :, :], raw[slot][:, :, par * P:(par + 1) * P], ACT.Copy).then_inc(hi_done, 1)

            def split_next(s, u):
                v = u + 1
                g = (s + 1 - (v % 2)) // 2 if isinstance(s, int) else None
                slot = (v // 2) % 2
                split(s + 1, slot, v % 2, (s - u) * 4 + 16 * (v // 4 + 1))

            def norm(nu_, pre=None):
                base = 8 * nu_
                groups = norm_tokens[nu_]
                for k in range(KC):
                    if nu_ == 0:
                        act.wait_ge(xT_lat, k + 1)
                        act.wait_ge(xT_ctx, k + 1)
                    elif k == 0:
                        act.wait_ge(drained, pre)
                    t0 = groups[-1][0].start
                    act.activation(sqb[:, k, t0:TOK], xT[:, k, t0:TOK], ACT.Square).then_inc(sq_ready, 1)
                act.wait_ge(ss_ready, nu_ + 1)
                for i, (cols, n, v) in enumerate(groups):
                    ins = act.activation(rstd[:, cols], pb[4 + i][:, 0:n], ACT.Ln, scale=1.0 / D, bias=eps[:, 0:1])
                ins.then_inc(sd_ready, 1)
                act.wait_ge(sd_ready, nu_ + 1)
                t0 = groups[-1][0].start
                act.activation(rstd[:, t0:TOK], rstd[:, t0:TOK], ACT.Exp, scale=-0.5).then_inc(rs_ready, 1)
                if nu_ == 4:
                    return
                layer, part = nu_ // 2, 3 * (nu_ % 2)
                for k in range(KC):
                    act.wait_ge(xn_ready, base + k + 1)
                    for cols, n, v in groups:
                        ins = act.activation(xn[:, k % 2, cols], xn[:, k % 2, cols], ACT.Identity,
                                             scale=wmod[:, nu_, k, v:v + 1], bias=gate(layer, part, k, v))
                    ins.then_inc(hm_ready, 1)
                    act.wait_ge(hm_ready, base + k + 1)
                    t0 = groups[-1][0].start
                    act.activation(hh[:, k, t0:TOK], xn[:, k % 2, t0:TOK], ACT.Copy).then_inc(hh_ready, 1)

            act.wait_ge(kon, 1)
            act.wait_ge(vec_ready, 2)
            act.activation(cT[:, :, :], vecT[:, 2, 0:16].rearrange("p (v k) -> p k v", v=2), ACT.Silu).then_inc(c_ready, 1)
            for k in range(KC):
                act.wait_ge(xin_t, k + 1)
                act.activation(xT[:, k, LATS], pb[2 * (k % 2)][:, :], ACT.Copy).then_inc(xT_lat, 1)
            split(0, 0, 0, 16)
            act.wait_ge(s_wg, 48)
            act.activation(wgh[:, :, :], wgr[:, :, :], ACT.Copy).then_inc(wg_hi, 1)
            norm(0)
            act.wait_ge(gv, 3)
            act.activation(gtmp[:, 2, :, :], gtmp[:, 1, :, :], ACT.Exp, scale=-1.0).then_inc(ga, 1)
            act.activation(sc32[:, 2, :], sc32[:, 0, :], ACT.Exp).then_inc(ga, 1)
            act.activation(gtmp[:, 3, :, :], gates[:, :, 16:32], ACT.Exp, scale=-1.0).then_inc(ga, 1)
            act.wait_ge(ga, 1)
            act.activation(gtmp[:, 2, :, :], gtmp[:, 2, :, :], ACT.Ln, bias=one[:, 0:1]).then_inc(ga, 1)
            act.wait_ge(gv, 10)
            act.activation(allsc[:, 1, :, :], allsc[:, 0, :, :], ACT.Exp).then_inc(ga, 1)
            act.activation(allsc[:, 2, :, :], gtmp[:, 0, :, :], ACT.Exp).then_inc(ga, 1)
            act.activation(allsc[:, 3, :, :].rearrange("p a b -> p (a b)"), pb[7][:, 96:192], ACT.Exp).then_inc(ga, 1)

            def silu_row(s, par):
                act.wait_ge(conv_step, 5 * s + 5)
                act.activation(row(qkv, s), cv[:, par, :], ACT.Silu).then_inc(silu_done, 1)

            def dnin(b, first=False, z=False):
                for u in range(4):
                    s = 4 * b + u
                    split_next(s, u)
                    if not (first and u == 0) and not (z and s > 24):
                        silu_row(s - 1, (u + 1) % 2)
                    act.wait_ge(proj_done, s + 1)
                    if z:
                        if s >= 26:
                            act.wait_ge(zs[u % 2], 16 * ((s - 24) // 2))
                        act.activation(zst[:, u % 2, CTXS], pb[2 * (u % 2) + 1][:, 0:CTX], ACT.Silu)
                        act.activation(zst[:, u % 2, LATS], pb[2 * (u % 2)][:, :], ACT.Silu).then_inc(drained, 1)
                        continue
                    if not first or u >= 2:
                        act.wait_ge(conv_step, 5 * (s - 1))
                    else:
                        act.wait_ge(pads, 2)
                    act.activation(xr[:, u % 2, 2:258], pb[2 * (u % 2) + 1][:, 0:CTX], ACT.Copy)
                    act.activation(xr[:, u % 2, 262:774], pb[2 * (u % 2)][:, :], ACT.Copy).then_inc(drained, 1)

            dnin(0, first=True)
            with act.Fori(1, 6) as b:
                dnin(b)
            dnin(6, z=True)
            dnin(7, z=True)

            def head(n, first=False):
                if first:
                    act.wait_ge(vs_ready, 1)
                else:
                    act.wait_ge(head_out, n)
                act.activation(l2b[:, 0, :], row(qkv, n), ACT.Square)
                act.activation(l2b[:, 1, :], row(qkv, 8 + n), ACT.Square).then_inc(l2_sq, 1)
                act.wait_ge(l2_ss, n + 1)
                for i in range(4):
                    ins = act.activation(l2b[:, i // 2, (i % 2) * 386:(i % 2 + 1) * 386], pb[i][:, 0:386], ACT.Ln, bias=eps[:, 0:1])
                ins.then_inc(l2_sd, 1)
                act.wait_ge(l2_sd, n + 1)
                act.activation(l2b[:, :, :], l2b[:, :, :], ACT.Exp, scale=-0.5).then_inc(l2_rc, 1)
                act.wait_ge(qk_ready, 2 * n + 2)
                for g in range(4):
                    act.wait_ge(x_ready, 4 * n + g + 1)
                    act.activation(qd[:, 3 * g:3 * g + 3, :].rearrange("p c i -> p (c i)"), pb[4 + g][:, 0:384], ACT.Exp).then_inc(eg_ready, 1)
                act.wait_ge(xm_ready, 2 * n + 1)
                act.activation(QKT[:, :, :], QKT[:, :, :], ACT.Exp).then_inc(dec_ready, 1)
                act.wait_ge(xm_ready, 2 * n + 2)
                act.activation(Am[:, :, :], Am[:, :, :], ACT.Exp, scale=-1.0).then_inc(dec_ready, 1)
                act.wait_ge(kv_t, n + 1)
                for i in range(4):
                    dst = (kN, vN)[i // 2][:, 3 * (i % 2):3 * (i % 2) + 3, :]
                    ins = act.activation(dst.rearrange("p c i -> p (c i)"), pb[i][:, 0:384], ACT.Copy)
                ins.then_inc(kv_nat, 1)
                for g in range(4):
                    act.wait_ge(tu_ready, 28 * n + 24 + g + 1)
                    for m in range(3 * g, 3 * g + 3):
                        ins = act.activation(TU[:, 1, m, :], TU[:, 1, m, :], ACT.Copy, scale=SC[:, 4, m // NT, m % NT:m % NT + 1])
                    ins.then_inc(ub_ready, 1)
                for t in range(NT):
                    for d in range(2):
                        c = ORDER[d][t]
                        act.wait_ge(nu_ps[d], NT * n + t + 1)
                        act.activation(nu[d][:, :], pb[4 * d + 1][:, 0:P], ACT.Copy).then_inc(nu_ready[d], 1)
                        act.activation(nuk[d][:, :], pb[4 * d + 1][:, 0:P], ACT.Copy, scale=SC[:, 2, d, c:c + 1]).then_inc(nu_ready[d], 1)

            head(0, first=True)
            with act.Fori(1, HEADS) as n:
                head(n)

            for h in range(HEADS):
                if h == 0:
                    act.wait_ge(head_out, HEADS)
                act.activation(qkv[:, 8 + h, 0:TOK], qkv[:, h, 0:TOK], ACT.Square).then_inc(f_sq, 1)
            for h in range(HEADS):
                act.wait_ge(f_ss, h + 1)
                for i in range(2):
                    ins = act.activation(qkv[:, 8 + h, 384 * i:384 * (i + 1)], pb[2 * (h % 4) + i][:, 0:384], ACT.Ln, scale=1.0 / P, bias=eps[:, 0:1])
                ins.then_inc(f_sd, 1)
                act.wait_ge(f_sd, h + 1)
                act.activation(qkv[:, 8 + h, 0:TOK], qkv[:, 8 + h, 0:TOK], ACT.Exp, scale=-0.5).then_inc(f_rc, 1)
            for h in range(HEADS):
                act.wait_ge(f_y, h + 1)
                act.activation(hh[:, h, :], qkv[:, h, 0:TOK], ACT.Copy).then_inc(y_hi, 1)

            for u in range(8):
                split_next(S_DNOUT + u, u % 4)
            norm(1, pre=S_MLP0)

            def mlp(layer, blk, last=False):
                groups = norm_tokens[1 + 2 * layer]
                t0 = groups[-1][0].start
                base = (S_MLP0, S_MLP1)[layer]
                for u in range(16):
                    s = base + 16 * blk + u
                    if not (last and u == 15):
                        split_next(s, u % 4)
                    if u < 8:
                        m = 32 * layer + 8 * blk + u
                        act.wait_ge(proj_done, s + 1)
                        if not (isinstance(m, int) and m < 2):
                            act.wait_ge(sq_done, m - 1)
                            act.wait_ge(hid_hi, m - 1)
                        for i, (cols, n, v) in enumerate(groups):
                            ins = act.activation(mtmp[:, u % 2, cols], pb[2 * (u % 2) + i][:, 0:n], ACT.Relu)
                        ins.then_inc(drained, 1)
                        act.wait_ge(drained, s + 1)
                        act.activation(hidh[:, u, t0:TOK], mtmp[:, u % 2, t0:TOK], ACT.Square).then_inc(hid_hi, 1)

            mlp(0, 0)
            with act.Fori(1, 4) as blk:
                mlp(0, blk)
            norm(2, pre=S_QKV)

            def qkvs(b, kind):
                for u in range(4):
                    s = S_QKV + 4 * b + u
                    split_next(s, u)
                    act.wait_ge(proj_done, s + 1)
                    lat = pb[2 * (u % 2)]
                    o = 4 * b + u
                    if kind == 2:
                        act.activation(row(vT, o - 16)[:, CTXS], pb[2 * (u % 2) + 1][:, 0:CTX], ACT.Copy)
                        act.activation(row(vT, o - 16)[:, LATS], lat[:, :], ACT.Copy).then_inc(drained, 1)
                        continue
                    if kind == 1:
                        act.activation(row(kT, o - 8)[:, CTXS], pb[2 * (u % 2) + 1][:, 0:CTX], ACT.Copy)
                        act.activation(row(kT, o - 8)[:, LATS], lat[:, :], ACT.Copy)
                    else:
                        act.activation(row(qT, o), lat[:, :], ACT.Copy)
                    if not (isinstance(o, int) and o < 2):
                        act.wait_ge(rp_sin, o - 1)
                    for q in range(4):
                        ins = act.activation(rsw[32 * q:32 * q + 32, u % 2, :], lat[32 * (q ^ 1):32 * (q ^ 1) + 32, :], ACT.Copy)
                    ins.then_inc(drained, 1)

            for b in range(6):
                qkvs(b, b // 2)

            act.wait_ge(lam_v, 2)
            act.activation(sc32[:, 3, 2:4], sc32[:, 3, 0:2], ACT.Exp).then_inc(lam_a, 1)

            def attend(h, first=False):
                if first:
                    act.wait_ge(qz_zero, 1)
                    act.wait_ge(drained, S_DAOUT)
                    act.wait_ge(rp_sin, 16)
                else:
                    act.wait_ge(s_ps, 8 * h)
                    act.wait_ge(vt_ps, h)
                act.activation(qz[0:64, 0, :], row(qT, h)[0:64, :], ACT.Copy)
                act.activation(qz[64:P, 1, :], row(qT, h)[64:P, :], ACT.Copy)
                act.activation(vs2[:, :], row(vT, h), ACT.Copy).then_inc(qz_ready, 1)
                act.wait_ge(vt_ps, h + 1)
                if not first:
                    act.wait_ge(at_ps, h)
                for i in range(2):
                    ins = act.activation(vn[:, 3 * i:3 * i + 3, :].rearrange("p c i -> p (c i)"), pb[i][:, 0:384], ACT.Copy)
                ins.then_inc(vn_ready, 1)
                for t in range(4):
                    for m in range(2):
                        e = 2 * t + m
                        act.wait_ge(nm_ready, 8 * h + e + 1)
                        if not (first and t < 2):
                            act.wait_ge(pc_ready, 4 * h + t - 1)
                        act.activation(pr[:, t % 2, m, :].rearrange("p (a k) -> p a k", a=2), sps[m][:, :, 0:384], ACT.Exp,
                                       scale=0.125, bias=ast[:, 2 + m, t:t + 1],
                                       accum_out=ast[:, 4 + m, t:t + 1]).then_inc(e_ready, 1)
                act.wait_ge(at_ps, h + 1)
                act.activation(osq[:, 0, :], pb[6][:, :], ACT.Square)
                act.activation(osq[:, 1, :], pb[6][:, :], ACT.Copy).then_inc(a_sq, 1)
                act.wait_ge(a_ss, h + 1)
                act.activation(orr[:, :], pb[7][:, :], ACT.Ln, scale=1.0 / P, bias=eps[:, 0:1]).then_inc(a_sd, 1)
                act.wait_ge(a_sd, h + 1)
                act.activation(orr[:, :], orr[:, :], ACT.Exp, scale=-0.5).then_inc(a_rc, 1)

            attend(0, first=True)
            with act.Fori(1, HEADS) as h:
                attend(h)
            for h in range(HEADS):
                if h == 0:
                    act.wait_ge(a_y, HEADS)
                act.activation(hh[:, h, LATS], qT[:, h, :], ACT.Copy).then_inc(y_hi, 1)
            for u in range(8):
                split_next(S_DAOUT + u, u % 4)
            norm(3, pre=S_MLP1)
            mlp(1, 0)
            with act.Fori(1, 3) as blk:
                mlp(1, blk)
            mlp(1, 3, last=True)
            norm(4, pre=S_END)
            for t in range(4):
                for i in range(2):
                    act.wait_ge(fin_ps, 2 * t + i + 1)
                    act.activation(fin[:, t, 512 * i:512 * (i + 1)], pb[(2 * t + i) % 4][:, :], ACT.Copy).then_inc(fin_ready, 1)

        @block.vector
        def _(dve):
            def split(s, slot, par):
                dve.wait_ge(hi_done, s + 1)
                dve.tensor_tensor(wlo[par][:, :, :], raw[slot][:, :, par * P:(par + 1) * P], whi[par][:, :, :],
                                  ALU.subtract).then_inc(lo_done, 1)

            def split_next(s, u):
                split(s + 1, ((u + 1) // 2) % 2, (u + 1) % 2)

            def norm(nu_):
                base = 8 * nu_
                groups = norm_tokens[nu_]
                t0 = groups[-1][0].start
                dve.wait_ge(rs_ready, nu_ + 1)
                if nu_ == 4:
                    for k in range(KC):
                        dve.scalar_tensor_tensor(sqb[:, k, LATS], xT[:, k, LATS], vecT[:, 1, 120 + k:121 + k], rstd[:, LATS],
                                                 op0=ALU.mult, op1=ALU.mult).then_inc(fin_n, 1)
                    return

                def low(k):
                    dve.wait_ge(hh_ready, base + k + 1)
                    dve.tensor_tensor(hl[:, k, t0:TOK], xn[:, k % 2, t0:TOK], hh[:, k, t0:TOK], ALU.subtract).then_inc(hl_ready, 1)

                for k in range(KC):
                    if k >= 2:
                        low(k - 2)
                        dve.wait_ge(hl_ready, base + k - 1)
                    dve.tensor_tensor(xn[:, k % 2, t0:TOK], xT[:, k, t0:TOK], rstd[:, t0:TOK], ALU.mult).then_inc(xn_ready, 1)
                low(6)
                low(7)

            chain = [0]

            def link(ins):
                chain[0] += 1
                ins.then_inc(gv, 1)
                dve.wait_ge(gv, chain[0])

            def take_mods(layer, c0, c1, bank_, first_tile, done):
                dve.wait_ge(ada_done, done)
                n = c1 - c0
                src = pb[bank_][:, 2 * c0:2 * c1].rearrange("p (c v) -> p c v", v=2)
                dve.tensor_tensor(mods[:, layer, c0:c1, :], src, bc(vecT[:, 0, 48 * layer + c0:48 * layer + c1], 2), ALU.add).then_inc(mod_ready, 1)

            def take_wmod(i, n_mod):
                layer, part = i // 2, 3 * (i % 2) + 1
                dve.wait_ge(mod_ready, n_mod)
                dve.scalar_tensor_tensor(wmod[:, i, :, :], mods[:, layer, part * KC:(part + 1) * KC, :], 1.0,
                                         bc(vecT[:, 0, 96 + 8 * i:104 + 8 * i], 2), op0=ALU.add, op1=ALU.mult).then_inc(a_mods, 1)
                dve.wait_ge(a_mods, i + 1)

            dve.wait_ge(vec_t, 1)
            dve.tensor_copy(vecT[:, 0:2, :].rearrange("p a n -> p (a n)"), pb[7][:, 0:256])
            dve.tensor_copy(vecT[:, 2, 0:18], pb[7][:, 256:274]).then_inc(vec_ready, 2)
            dve.wait_ge(vec_ready, 2)
            for k in range(KC):
                dve.wait_ge(xin_t, k + 1)
                dve.tensor_copy(xT[:, k, CTXS], pb[2 * (k % 2) + 1][:, 0:CTX]).then_inc(xT_ctx, 1)
            split(0, 0, 0)
            dve.wait_ge(wg_hi, 1)
            dve.tensor_tensor(wgl[:, :, :], wgr[:, :, :], wgh[:, :, :], ALU.subtract).then_inc(wg_lo, 1)
            take_mods(0, 0, 16, 6, 0, 16)
            take_wmod(0, 1)
            norm(0)

            dve.wait_ge(gate_ps, 1)
            link(dve.tensor_copy(gates[:, :, :].rearrange("p a b -> p (a b)"), pb[7][:, 0:192]))
            link(dve.tensor_tensor(gtmp[:, 0, :, :], gates[:, :, 0:16], over(sc32[:, 1, :], NT), ALU.add))
            link(dve.scalar_tensor_tensor(gtmp[:, 1, :, :], gtmp[:, 0, :, :], -1.0, gtmp[:, 0, :, :], op0=ALU.mult, op1=ALU.max))
            dve.wait_ge(ga, 4)
            link(dve.tensor_scalar(gtmp[:, 1, :, :], gtmp[:, 0, :, :], 0.0, None, ALU.max))
            link(dve.tensor_tensor(gtmp[:, 1, :, :], gtmp[:, 1, :, :], gtmp[:, 2, :, :], ALU.add))
            link(dve.scalar_tensor_tensor(gdec[:, :, :], gtmp[:, 1, :, :], -1.0, over(sc32[:, 2, :], NT), op0=ALU.mult, op1=ALU.mult))
            link(dve.tensor_scalar(gtmp[:, 3, :, :], gtmp[:, 3, :, :], 1.0, None, ALU.add))
            link(dve.reciprocal(allsc[:, 4, :, :], gtmp[:, 3, :, :]))
            dve.wait_ge(gp, 1)
            link(dve.tensor_copy(allsc[:, 0, :, :].rearrange("p t (d h) -> p d t h", d=2),
                                 pb[7][:, 0:96].rearrange("p (d t h) -> p d t h", d=2, t=NT)))
            link(dve.tensor_tensor(gtmp[:, 0, :, :].rearrange("p a b -> p (a b)"), pb[7][:, 96:192],
                                   allsc[:, 0, :, :].rearrange("p a b -> p (a b)"), ALU.subtract))
            dve.wait_ge(ga, 7)
            dve.tensor_scalar(allsc[:, 1, :, :], allsc[:, 1, :, :], -1.0, None, ALU.mult).then_inc(sc_all, 1)

            def dnin(b, first=False, z=False):
                for u in range(4):
                    s = 4 * b + u
                    split_next(s, u)
                    if z:
                        continue
                    dve.wait_ge(drained, s + 1)
                    if not first or u >= 2:
                        dve.wait_ge(silu_done, s - 1)
                    dve.tensor_scalar(cv[:, u % 2, :], xr[:, u % 2, 0:SLOT], vecT[:, 1, ds(s)], None, ALU.mult).then_inc(conv_step, 1)
                    for w in range(1, 5):
                        dve.wait_ge(conv_step, 5 * s + w)
                        dve.scalar_tensor_tensor(cv[:, u % 2, :], xr[:, u % 2, w:w + SLOT], vecT[:, 1, ds(24 * w + s)], cv[:, u % 2, :],
                                                 op0=ALU.mult, op1=ALU.add).then_inc(conv_step, 1)

            dnin(0, first=True)
            with dve.Fori(1, 6) as b:
                dnin(b)
            dnin(6, z=True)
            dnin(7, z=True)
            take_mods(0, 16, 48, 6, 16, 48)
            take_wmod(1, 2)

            def head(n, first=False):
                dve.wait_ge(vs_ready, n + 1)
                dve.wait_ge(l2_rc, n + 1)
                dve.scalar_tensor_tensor(qS[:, :], l2b[:, 0, :], float(P) ** -0.5, row(qkv, n), op0=ALU.mult, op1=ALU.mult).then_inc(qk_ready, 1)
                dve.tensor_tensor(kS[:, :], l2b[:, 1, :], row(qkv, 8 + n), ALU.mult).then_inc(qk_ready, 1)
                dve.wait_ge(sc_ready, n + 1)
                for g in range(4):
                    dve.wait_ge(grow_ps, 4 * n + g + 1)
                    dve.tensor_tensor(Am[:, 3 * g:3 * g + 3, :], pb[4 + g][:, 0:384].rearrange("p (c i) -> p c i", i=P),
                                      bc(SC[:, 0, g // 2, 3 * (g % 2):3 * (g % 2) + 3], P), ALU.subtract).then_inc(x_ready, 1)
                dve.wait_ge(x_ready, 4 * n + 4)
                dve.tensor_scalar(QKT[:, :, :], Am[:, :, :], 0.0, None, ALU.min).then_inc(xm_ready, 1)
                dve.wait_ge(xm_ready, 2 * n + 1)
                dve.tensor_scalar(Am[:, :, :], Am[:, :, :], 0.0, None, ALU.max).then_inc(xm_ready, 1)
                dve.wait_ge(qk_ready, 2 * n + 2)
                dve.wait_ge(eg_ready, 4 * n + 4)
                for d in range(2):
                    dve.tensor_tensor(qd[:, NT * d:NT * d + 2, :], qd[:, NT * d:NT * d + 2, :], chunks(qS, 0, 2), ALU.mult)
                    ins = dve.tensor_tensor(qd[:, NT * d + 2:NT * d + 6, :], qd[:, NT * d + 2:NT * d + 6, :], chunks(qS, 2, 4), ALU.mult)
                ins.then_inc(qd_ready, 1)
                dve.wait_ge(kk_ps, n + 1)
                dve.wait_ge(dec_ready, 2 * n + 2)
                for g in range(4):
                    dve.tensor_tensor(Am[:, 3 * g:3 * g + 3, :].rearrange("p c i -> p (c i)"), pb[4 + g % 2][:, 0:384],
                                      Am[:, 3 * g:3 * g + 3, :].rearrange("p c i -> p (c i)"), ALU.mult).then_inc(am_step, 1)
                dve.wait_ge(am_step, 5 * n + 4)
                for m in range(NM):
                    ins = dve.scalar_tensor_tensor(Am[:, m, :], Am[:, m, :], SC[:, 4, m // NT, m % NT:m % NT + 1], STRICT[m // NT],
                                                   op0=ALU.mult, op1=ALU.mult)
                ins.then_inc(am_step, 1)
                dve.wait_ge(qk_ps, n + 1)
                for g in range(4):
                    dve.tensor_tensor(QKT[:, 3 * g:3 * g + 3, :].rearrange("p c i -> p (c i)"), pb[6 + g % 2][:, 0:384],
                                      QKT[:, 3 * g:3 * g + 3, :].rearrange("p c i -> p (c i)"), ALU.mult).then_inc(qkt_step, 1)
                dve.wait_ge(qkt_step, 6 * n + 4)
                for d in range(2):
                    dve.tensor_tensor(QKT[:, NT * d:NT * (d + 1), :], QKT[:, NT * d:NT * (d + 1), :], over(CUM[d], NT), ALU.mult).then_inc(qkt_step, 1)
                if first:
                    dve.wait_ge(s_lvl, 16)
                for level in range(LEVELS):
                    for g in range(4):
                        dve.wait_ge(p_ps, 28 * n + 4 * level + g + 1)
                        dve.tensor_tensor(Pm[:, 3 * g:3 * g + 3, :], pb[g][:, 0:384].rearrange("p (c i) -> p c i", i=P),
                                          over(lvl[:, g // 2, level, :], 3), ALU.mult).then_inc(p_ready, 1)
                    for g in range(4):
                        dve.wait_ge(x_ps, 28 * n + 4 * level + g + 1)
                        if level < LEVELS - 1:
                            t = tu_ap(g, level)
                            src = pb[4 + g][:, 0:384].rearrange("p (a b c) -> p a b c", a=2, c=1 << level)
                            dve.tensor_tensor(t, t, src, ALU.subtract).then_inc(tu_ready, 1)
                        else:
                            t = TU[:, 1, 3 * g:3 * g + 3, :][:, :, 64 * (1 - g // 2):64 * (2 - g // 2)]
                            dve.tensor_tensor(t, t, pb[4 + g][:, 192:384].rearrange("p (m c) -> p m c", m=3), ALU.subtract).then_inc(tu_ready, 1)
                for d in range(2):
                    dve.memset(St[d][:, :], 0.0).then_inc(s_new[d], 1)
                seen = {}
                for t in range(NT):
                    for d in range(2):
                        c = ORDER[d][t]
                        dve.wait_ge(ks_ps[d], NT * n + t + 1)
                        dve.scalar_tensor_tensor(rr[d][:, :], pb[4 * d][:, 0:P], SC[:, 1, d, c:c + 1], vN[:, c, :],
                                                 op0=ALU.mult, op1=ALU.add).then_inc(r_ready[d], 1)
                    for d in range(2):
                        c = ORDER[d][t]
                        dve.wait_ge(ds_ps[d], NT * n + t + 1)
                        dve.wait_ge(o_ps[d], NT * n + t + 1)
                        dve.wait_ge(s_new[d], 7 * n + t + 1)
                        dve.scalar_tensor_tensor(St[d][:, :], St[d][:, :], SC[:, 3, d, c:c + 1], pb[4 * d + 3][:, 0:P],
                                                 op0=ALU.mult, op1=ALU.add).then_inc(s_new[d], 1)
                        o = OB[:, c * P:(c + 1) * P]
                        if c in seen:
                            dve.wait_ge(o_sum[1 - d], NT * n + seen[c] + 1)
                            dve.tensor_tensor(o, pb[4 * d + 2][:, 0:P], o, ALU.add).then_inc(o_sum[d], 1)
                        else:
                            dve.tensor_copy(o, pb[4 * d + 2][:, 0:P]).then_inc(o_sum[d], 1)
                            seen[c] = t
                for d in range(2):
                    dve.wait_ge(o_sum[d], NT * n + NT)
                dve.tensor_scalar(qkv[:, ds(n), 0:TOK].rearrange("p a n -> p (a n)"), OB[:, 0:TOK], 1.0, None, ALU.mult).then_inc(head_out, 1)

            head(0, first=True)
            with dve.Fori(1, HEADS) as n:
                head(n)

            def y_low(h):
                dve.wait_ge(y_hi, h + 1)
                dve.tensor_tensor(hl[:, h, :], qkv[:, h, 0:TOK], hh[:, h, :], ALU.subtract).then_inc(y_lo, 1)

            dve.wait_ge(s_zin, 16)
            for h in range(HEADS):
                r = qkv[:, 8 + h, 0:TOK]
                dve.wait_ge(f_rc, h + 1)
                dve.scalar_tensor_tensor(r, qkv[:, h, 0:TOK], vecT[:, 2, 16:17], r, op0=ALU.mult, op1=ALU.mult).then_inc(f_y1, 1)
                dve.wait_ge(f_y1, h + 1)
                dve.tensor_tensor(qkv[:, h, 0:TOK], r, zin[:, h, :], ALU.mult).then_inc(f_y, 1)
                if h:
                    y_low(h - 1)
            y_low(HEADS - 1)

            def residual(s, o, u, layer, part, groups):
                dve.wait_ge(proj_done, s + 1)
                dve.wait_ge(drained, s)
                for i, (cols, n, v) in enumerate(groups):
                    x = xT[:, o, cols]
                    ins = dve.scalar_tensor_tensor(x, pb[2 * (u % 2) + i][:, 0:n], gate(layer, part, o, v), x, op0=ALU.mult, op1=ALU.add)
                ins.then_inc(drained, 1)

            for u in range(8):
                split_next(S_DNOUT + u, u % 4)
                residual(S_DNOUT + u, u, u, 0, 2, GROUPS)
            norm(1)

            def mlp(layer, blk, last=False):
                groups = norm_tokens[1 + 2 * layer]
                t0 = groups[-1][0].start
                base = (S_MLP0, S_MLP1)[layer]
                for u in range(16):
                    s = base + 16 * blk + u
                    if not (last and u == 15):
                        split_next(s, u % 4)
                    if u < 8:
                        m = 32 * layer + 8 * blk + u
                        dve.wait_ge(drained, s + 1)
                        if not (isinstance(m, int) and m < 2):
                            dve.wait_ge(hid_lo, m - 1)
                        dve.tensor_tensor(msq[:, u % 2, t0:TOK], mtmp[:, u % 2, t0:TOK], mtmp[:, u % 2, t0:TOK], ALU.mult).then_inc(sq_done, 1)
                        dve.wait_ge(sq_done, m + 1)
                        dve.wait_ge(hid_hi, m + 1)
                        dve.tensor_tensor(hidl[:, u, t0:TOK], msq[:, u % 2, t0:TOK], hidh[:, u, t0:TOK], ALU.subtract).then_inc(hid_lo, 1)
                    else:
                        residual(s, u - 8, u, layer, 5, groups)

            mlp(0, 0)
            with dve.Fori(1, 4) as blk:
                mlp(0, blk)
            take_mods(1, 0, 48, 7, 0, 96)
            take_wmod(2, 3)
            take_wmod(3, 3)
            norm(2)

            dve.wait_ge(s_rope, 32)
            dve.tensor_tensor(lamb[:, :, 0, :], lamb[:, :, 0, :], lamb[:, :, 1, :], ALU.mult).then_inc(lam_v, 1)
            dve.wait_ge(lam_v, 1)
            dve.tensor_reduce(sc32[:, 3, 0:2], lamb[:, :, 0, :], AX_X, ALU.add).then_inc(lam_v, 1)

            def qkvs(b, kind):
                for u in range(4):
                    s = S_QKV + 4 * b + u
                    split_next(s, u)
                    if kind == 2:
                        continue
                    o = 4 * b + u
                    r = row(qT, o) if kind == 0 else row(kT, o - 8)[:, LATS]
                    dve.wait_ge(drained, s + 1)
                    if o:
                        dve.wait_ge(rp_sin, o)
                    dve.tensor_tensor(rcs[:, :], r, ropt[:, 0, :], ALU.mult).then_inc(rp_cos, 1)
                    dve.tensor_tensor(rsw[:, u % 2, :], rsw[:, u % 2, :], ropt[:, 1, :], ALU.mult).then_inc(rp_sw, 1)
                    dve.wait_ge(rp_cos, o + 1)
                    dve.wait_ge(rp_sw, o + 1)
                    dve.tensor_tensor(r, rcs[:, :], rsw[:, u % 2, :], ALU.add).then_inc(rp_sin, 1)

            for b in range(6):
                qkvs(b, b // 2)
            dve.wait_ge(rp_sin, 16)
            dve.wait_ge(proj_done, S_DAOUT)
            for m in range(2):
                ins = dve.memset(qz[64 * (1 - m):64 * (2 - m), m, :], 0.0)
            ins.then_inc(qz_zero, 1)
            dve.wait_ge(lam_a, 1)
            dve.tensor_tensor(sc32[:, 3, 4:5], sc32[:, 3, 3:4], sc32[:, 3, 2:3], ALU.subtract).then_inc(lam_v, 1)
            dve.wait_ge(lam_v, 3)
            dve.tensor_scalar(sc32[:, 3, 5:6], sc32[:, 3, 4:5], -LAMBDA_INIT, None, ALU.add).then_inc(lam_v, 1)
            dve.tensor_scalar(sc32[:, 3, 6:7], vecT[:, 2, 17:18], 1.0 - LAMBDA_INIT, None, ALU.mult).then_inc(lam_v, 1)
            dve.wait_ge(lam_v, 5)

            def attend(h, first=False):
                for t in range(5):
                    if t < 4:
                        for m in range(2):
                            e = 8 * h + 2 * t + m
                            dve.wait_ge(s_ps, e + 1)
                            dve.tensor_reduce(ast[:, m, t:t + 1], sps[m][:, :, 0:384], mybir.AxisListType.XY, ALU.max).then_inc(mx_ready, 1)
                            dve.wait_ge(mx_ready, e + 1)
                            dve.tensor_scalar(ast[:, 2 + m, t:t + 1], ast[:, m, t:t + 1], -0.125, None, ALU.mult).then_inc(nm_ready, 1)
                    if t >= 1:
                        r, q = t - 1, (t - 1) % 2
                        dve.wait_ge(e_ready, 8 * h + 2 * r + 2)
                        dve.reciprocal(ast[:, 6:8, r:r + 1], ast[:, 4:6, r:r + 1]).then_inc(rl_ready, 1)
                        dve.wait_ge(rl_ready, 8 * h + 2 * r + 1)
                        dve.tensor_scalar(ast[:, 7, r:r + 1], ast[:, 7, r:r + 1], sc32[:, 3, 5:6], None, ALU.mult).then_inc(rl_ready, 1)
                        dve.tensor_scalar(pr[:, q, 0, :], pr[:, q, 0, :], ast[:, 6, r:r + 1], None, ALU.mult).then_inc(p0_ready, 1)
                        dve.wait_ge(rl_ready, 8 * h + 2 * r + 2)
                        dve.wait_ge(p0_ready, 4 * h + r + 1)
                        if not (first and r < 2):
                            dve.wait_ge(pt_ps, 4 * h + r - 1)
                        dve.scalar_tensor_tensor(pc[:, q, :], pr[:, q, 1, :], ast[:, 7, r:r + 1], pr[:, q, 0, :],
                                                 op0=ALU.mult, op1=ALU.add).then_inc(pc_ready, 1)
                        dve.wait_ge(pt_ps, 4 * h + r + 1)
                        if r == 0 and not first:
                            dve.wait_ge(at_ps, h)
                        for i in range(2):
                            ins = dve.tensor_copy(pT[:, 3 * i:3 * i + 3, r * P:(r + 1) * P], pb[i][:, 0:384].rearrange("p (c i) -> p c i", i=P))
                        ins.then_inc(pT_ready, 1)
                dve.wait_ge(a_rc, h + 1)
                dve.scalar_tensor_tensor(row(qT, h), osq[:, 1, :], sc32[:, 3, 6:7], orr[:, :], op0=ALU.mult, op1=ALU.mult).then_inc(a_y, 1)

            attend(0, first=True)
            with dve.Fori(1, HEADS) as h:
                attend(h)
            for h in range(HEADS):
                dve.wait_ge(y_hi, 8 + h + 1)
                dve.tensor_tensor(hl[:, h, LATS], qT[:, h, :], hh[:, h, LATS], ALU.subtract).then_inc(y_lo, 1)
            for u in range(8):
                split_next(S_DAOUT + u, u % 4)
                residual(S_DAOUT + u, u, u, 1, 2, GROUPS[:1])
            norm(3)
            mlp(1, 0)
            with dve.Fori(1, 3) as blk:
                mlp(1, blk)
            mlp(1, 3, last=True)
            norm(4)

        @block.tensor
        def _(pe):
            def matmul3(u, hi, lo, groups, s, chunk_ready=None, count=0):
                pe.wait_ge(lo_done, s + 1)
                if not (isinstance(s, int) and s < 2):
                    pe.wait_ge(drained, s - 1)
                for k in range(KC):
                    if chunk_ready is not None:
                        pe.wait_ge(chunk_ready, count + k + 1)
                    for j, (w, x) in enumerate(((whi, hi), (whi, lo), (wlo, hi))):
                        for i, (cols, n, v) in enumerate(groups):
                            ins = pe.matmul(pb[2 * (u % 2) + i][:, 0:n], w[u % 2][:, k, :], x[:, k, cols],
                                            start=(k == 0 and j == 0), stop=(k == KC - 1 and j == 2))
                ins.then_inc(proj_done, 1)

            def ada(a, par, nth, bank_, tile):
                pe.wait_ge(s_ada[par], nth)
                for k in range(KC):
                    ins = pe.matmul(pb[bank_][:, ds(2 * tile, 2)], adaw[par][:, k, :], cT[:, k, :], start=(k == 0), stop=(k == KC - 1))
                ins.then_inc(ada_done, 1)

            def norm(nu_):
                for k in range(KC):
                    pe.wait_ge(sq_ready, 8 * nu_ + k + 1)
                    for i, (cols, n, v) in enumerate(norm_tokens[nu_]):
                        ins = pe.matmul(pb[4 + i][:, 0:n], ones, sqb[:, k, cols], start=(k == 0), stop=(k == KC - 1))
                ins.then_inc(ss_ready, 1)

            pe.wait_ge(s_cst, 16)
            pe.wait_ge(s_vec, 144)
            pe.transpose(pb[7][:, 0:P], vecR[:, 0, :], ident)
            pe.transpose(pb[7][:, P:2 * P], vecR[:, 1, :], ident)
            pe.transpose(pb[7][:, 2 * P:2 * P + 18], vecR[0:18, 2, :], cst[0:18, 0, 0:18]).then_inc(vec_t, 1)
            pe.wait_ge(s_x, 32)
            for k in range(KC):
                if k >= 2:
                    pe.wait_ge(xT_lat, k - 1)
                    pe.wait_ge(xT_ctx, k - 1)
                for t in range(NT):
                    dst = pb[2 * (k % 2) + 1][:, t * P:(t + 1) * P] if t < 2 else pb[2 * (k % 2)][:, (t - 2) * P:(t - 1) * P]
                    ins = pe.transpose(dst, xin[:, t, k * P:(k + 1) * P], ident)
                ins.then_inc(xin_t, 1)
            pe.wait_ge(c_ready, 1)
            with pe.Fori(0, 8) as i:
                for j in range(2):
                    ada(2 * i + j, j, 16 * (i + 1), 6, 2 * i + j)
            norm(0)
            pe.wait_ge(hl_ready, 8)
            pe.wait_ge(wg_lo, 1)
            for t in range(NT):
                for k in range(KC):
                    for j, (x, w) in enumerate(((hh, wgh), (hl, wgh), (hh, wgl))):
                        ins = pe.matmul(pb[7][:, 32 * t:32 * (t + 1)], x[:, k, t * P:(t + 1) * P], w[:, k, :],
                                        start=(k == 0 and j == 0), stop=(k == KC - 1 and j == 2))
            ins.then_inc(gate_ps, 1)

            def dnin(b, first=False):
                for u in range(4):
                    s = 4 * b + u
                    matmul3(u, hh, hl, GROUPS, s)
                    if first and u == 0:
                        pe.wait_ge(gv, 6)
                        for d in range(2):
                            pe.matmul(pb[7][:, 48 * d:48 * (d + 1)], CUM[d], gdec[:, :, 8 * d:8 * d + 8], start=True, stop=True)
                        pe.matmul(pb[7][:, 96:192], ones, gdec[:, :, :], start=True, stop=True).then_inc(gp, 1)
                    ada(16 + s, u % 2, (s - u) * 8 + 16 * (u // 2 + 9), 6, 16 + s)

            dnin(0, first=True)
            with pe.Fori(1, 8) as b:
                dnin(b)

            def head(n, first=False):
                pe.wait_ge(l2_sq, n + 1)
                if first:
                    pe.wait_ge(drained, S_DNOUT)
                    pe.wait_ge(mod_ready, 2)
                for i in range(4):
                    ins = pe.matmul(pb[i][:, 0:386], ones, l2b[:, i // 2, (i % 2) * 386:(i % 2 + 1) * 386], start=True, stop=True)
                ins.then_inc(l2_ss, 1)
                for g in range(4):
                    pe.wait_ge(gu_ready, 2 * n + g // 2 + 1)
                    pe.matmul(pb[4 + g][:, 0:384], ones, Pm[:, 3 * g:3 * g + 3, :].rearrange("p c i -> p (c i)"), start=True, stop=True).then_inc(grow_ps, 1)
                pe.wait_ge(qk_ready, 2 * n + 2)
                for c in range(NT):
                    pe.transpose(pb[c // 3][:, (c % 3) * P:(c % 3 + 1) * P], kS[:, off(c):off(c) + P], ident)
                for c in range(NT):
                    ins = pe.transpose(pb[2 + c // 3][:, (c % 3) * P:(c % 3 + 1) * P], vS[:, off(c):off(c) + P], ident)
                ins.then_inc(kv_t, 1)
                pe.wait_ge(eg_ready, 4 * n + 4)
                for c in range(NT):
                    k = kS[:, off(c):off(c) + P]
                    ins = pe.matmul(pb[4 + c // 3][:, (c % 3) * P:(c % 3 + 1) * P], k, k, start=True, stop=True)
                ins.then_inc(kk_ps, 1)
                for c in range(NT):
                    ins = pe.matmul(pb[6 + c // 3][:, (c % 3) * P:(c % 3 + 1) * P], kS[:, off(c):off(c) + P], qS[:, off(c):off(c) + P], start=True, stop=True)
                ins.then_inc(qk_ps, 1)
                for level in range(LEVELS):
                    s = 1 << level
                    for g in range(4):
                        if level == 0 and g == 0:
                            pe.wait_ge(am_step, 5 * n + 5)
                            pe.wait_ge(tu_init, n + 1)
                            pe.wait_ge(kv_nat, n + 1)
                        elif level:
                            pe.wait_ge(tu_ready, 28 * n + 4 * (level - 1) + g + 1)
                        for j in range(3):
                            m = 3 * g + j
                            ins = pe.matmul(pb[g][:, j * P:(j + 1) * P], Am[:, m, :], TU[:, 1, m, :], start=True, stop=True)
                        ins.then_inc(p_ps, 1)
                    if level == 0:
                        pe.wait_ge(qkt_step, 6 * n + 4)
                    for g in range(4):
                        pt, pu = ((0, 1), (1, 0))[g // 2]
                        pe.wait_ge(p_ready, 28 * n + 4 * level + g + 1)
                        for j in range(3):
                            m = 3 * g + j
                            if level < LEVELS - 1:
                                pe.matmul(pb[4 + g][:, 64 * j:64 * (j + 1)].rearrange("p (b c) -> p b c", c=s), Pm[:, m, :],
                                          half(TU[:, 0, m, :], s, pt), start=True, stop=True)
                            ins = pe.matmul(pb[4 + g][:, 192 + 64 * j:192 + 64 * (j + 1)].rearrange("p (b c) -> p b c", c=s), TU[:, 0, m, :],
                                            half(Pm[:, m, :], s, pu), start=True, stop=True)
                        ins.then_inc(x_ps, 1)
                pe.wait_ge(ub_ready, 4 * n + 4)
                pe.wait_ge(qkt_step, 6 * n + 6)
                pe.wait_ge(qd_ready, n + 1)
                for t in range(NT):
                    for d in range(2):
                        c = ORDER[d][t]
                        pe.wait_ge(s_new[d], 7 * n + t + 1)
                        pe.matmul(pb[4 * d][:, 0:P], kS[:, off(c):off(c) + P], St[d][:, :], start=True, stop=True).then_inc(ks_ps[d], 1)
                        if t:
                            pe.wait_ge(o_sum[d], NT * n + t)
                        pe.matmul(pb[4 * d + 2][:, 0:P], St[d][:, :], qd[:, NT * d + c, :], start=True, stop=False)
                    for d in range(2):
                        c = ORDER[d][t]
                        pe.wait_ge(r_ready[d], NT * n + t + 1)
                        pe.matmul(pb[4 * d + 1][:, 0:P], TU[:, 1, NT * d + c, :], rr[d][:, :], start=True, stop=True).then_inc(nu_ps[d], 1)
                    for d in range(2):
                        c = ORDER[d][t]
                        pe.wait_ge(nu_ready[d], 2 * (NT * n + t) + 1)
                        pe.matmul(pb[4 * d + 2][:, 0:P], nu[d][:, :], QKT[:, NT * d + c, :], start=False, stop=True).then_inc(o_ps[d], 1)
                        pe.wait_ge(nu_ready[d], 2 * (NT * n + t) + 2)
                        pe.matmul(pb[4 * d + 3][:, 0:P], kN[:, c, :], nuk[d][:, :], start=True, stop=True).then_inc(ds_ps[d], 1)

            head(0, first=True)
            with pe.Fori(1, HEADS) as n:
                head(n)
            for h in range(HEADS):
                pe.wait_ge(f_sq, h + 1)
                if h >= 4:
                    pe.wait_ge(f_sd, h - 3)
                for i in range(2):
                    ins = pe.matmul(pb[2 * (h % 4) + i][:, 0:384], ones, qkv[:, 8 + h, 384 * i:384 * (i + 1)], start=True, stop=True)
                ins.then_inc(f_ss, 1)
            for u in range(8):
                matmul3(u, hh, hl, GROUPS, S_DNOUT + u, None if u else y_lo, 0)
            norm(1)

            def mlp(layer, blk):
                groups = norm_tokens[1 + 2 * layer]
                base = (S_MLP0, S_MLP1)[layer]
                for u in range(16):
                    s = base + 16 * blk + u
                    if u == 0:
                        matmul3(u, hh, hl, groups, s, hl_ready, 8 + 16 * layer)
                    elif u < 8:
                        matmul3(u, hh, hl, groups, s)
                    elif u == 8:
                        matmul3(u, hidh, hidl, groups, s, hid_lo, 32 * layer + 8 * blk)
                    else:
                        matmul3(u, hidh, hidl, groups, s)
                    if layer == 0 and u < 12:
                        tile = 12 * blk + u
                        ada(48 + tile, u % 2, 96 * blk + 16 * (25 + u // 2), 7, tile)

            with pe.Fori(0, 4) as blk:
                mlp(0, blk)
            norm(2)
            for b in range(6):
                for u in range(4):
                    matmul3(u, hh, hl, GROUPS[:1] if b < 2 else GROUPS, S_QKV + 4 * b + u, hl_ready if b + u == 0 else None, 16)

            def attend(h, first=False):
                pe.wait_ge(qz_ready, h + 1)
                if first:
                    pe.wait_ge(drained, S_DAOUT)
                else:
                    pe.wait_ge(pT_ready, 4 * h)
                for c in range(NT):
                    ins = pe.transpose(pb[c // 3][:, (c % 3) * P:(c % 3 + 1) * P], vs2[:, c * P:(c + 1) * P], ident)
                ins.then_inc(vt_ps, 1)

                def scores(t):
                    for m in range(2):
                        if not (first and t == 0):
                            pe.wait_ge(e_ready, 8 * h + 2 * t + m - 1)
                        for i in range(2):
                            ins = pe.matmul(sps[m][:, i, 0:384], qz[:, m, t * P:(t + 1) * P], row(kT, h)[:, 384 * i:384 * (i + 1)], start=True, stop=True)
                        ins.then_inc(s_ps, 1)

                scores(0)
                for t in range(4):
                    if t < 3:
                        scores(t + 1)
                    pe.wait_ge(pc_ready, 4 * h + t + 1)
                    if t == 0:
                        pe.wait_ge(vn_ready, h + 1)
                    else:
                        pe.wait_ge(pT_ready, 4 * h + t)
                    for c in range(NT):
                        ins = pe.transpose(pb[c // 3][:, (c % 3) * P:(c % 3 + 1) * P], pc[:, t % 2, c * P:(c + 1) * P], ident)
                    ins.then_inc(pt_ps, 1)
                pe.wait_ge(pT_ready, 4 * h + 4)
                for c in range(NT):
                    ins = pe.matmul(pb[6][:, :], vn[:, c, :], pT[:, c, :], start=(c == 0), stop=(c == NT - 1))
                ins.then_inc(at_ps, 1)
                pe.wait_ge(a_sq, h + 1)
                pe.matmul(pb[7][:, :], ones, osq[:, 0, :], start=True, stop=True).then_inc(a_ss, 1)

            attend(0, first=True)
            with pe.Fori(1, HEADS) as h:
                attend(h)
            for u in range(8):
                matmul3(u, hh, hl, GROUPS[:1], S_DAOUT + u, None if u else y_lo, 8)
            norm(3)
            with pe.Fori(0, 4) as blk:
                mlp(1, blk)
            norm(4)
            pe.wait_ge(fin_n, 8)
            for t in range(4):
                for i in range(2):
                    j = 2 * t + i
                    if j >= 4:
                        pe.wait_ge(fin_ready, j - 3)
                    for k in range(4):
                        ins = pe.transpose(pb[j % 4][:, k * P:(k + 1) * P], sqb[:, 4 * i + k, CTX + t * P:CTX + (t + 1) * P], ident)
                    ins.then_inc(fin_ps, 1)


_INS = ["x", "c", "ctx", "c_ctx", "ada_w", "ada_b", "norm_w", "mlp_w1", "mlp_w2", "dn_w_in", "dn_conv", "dn_a_log",
        "dn_dt_bias", "dn_out_norm", "dn_w_out", "da_w_qkv", "da_lambda", "da_subln", "da_w_out", "final_norm"]


def kernel(**inputs):
    import concourse.bacc as _bacc
    from concourse.bass_utils import run_bass_kernel_spmd as _run

    nc = _bacc.Bacc("TRN2", target_bir_lowering=False, num_devices=1)
    arrays, args = {}, {}
    cst, lvl, rope = constants()
    for name, a in [(n, np.ascontiguousarray(inputs[n])) for n in _INS] + [("cst", cst), ("lvl", lvl), ("rope", rope)]:
        arrays[f"in_{name}"] = a
        args[name] = nc.dram_tensor(f"in_{name}", a.shape, mybir.dt.from_np(a.dtype), kind="ExternalInput").ap()
    args["out"] = nc.dram_tensor("out_0", (1, LAT, D), F32, kind="ExternalOutput").ap()
    build(nc, args)
    r = _run(nc, [arrays], core_ids=[0])
    return r.results[0]["out_0"]
```

```python
from contextlib import ExitStack

import numpy as np

import concourse.bass as bass
from concourse import mybir

F32 = mybir.dt.float32
F32R = mybir.dt.float32r
ACT = mybir.ActivationFunctionType
ALU = mybir.AluOpType
AX_X = mybir.AxisListType.X

P = 128
D = 1024
KC = D // P
CTX, LAT = 256, 512
TOK = CTX + LAT
NT = TOK // P
HEADS = 8
SLOT = TOK + 4
EPS = 1e-6
LAMBDA_INIT = float(0.8 - 0.6 * np.exp(-0.3))
LEVELS = 7
NM = 2 * NT
LATS, CTXS = slice(CTX, TOK), slice(0, CTX)
GROUPS = ((LATS, LAT, 0), (CTXS, CTX, 1))
S_DNIN, S_DNOUT, S_MLP0, S_QKV, S_DAOUT, S_MLP1, S_END = 0, 32, 40, 104, 128, 136, 200
ORDER = (tuple(range(NT)), (1, 0, 5, 4, 3, 2))


def off(c):
    return P * c + (4 if c >= 2 else 0)


def constants():
    p, f = np.indices((P, P))
    tri = [p == f, p >= 0, p <= f, p >= f, p > f, p < f]
    masks = []
    for d in range(2):
        for level in range(LEVELS):
            s = 1 << level
            m = (p // (2 * s) == f // (2 * s)) & ((p // s) % 2 == 0) & ((f // s) % 2 == 1)
            masks.append(m if d == 0 else m.T)
    cst = np.concatenate([x.astype(np.float32) for x in tri], axis=1)
    lvl = np.concatenate([x.astype(np.float32) for x in masks], axis=1)
    n = np.arange(LAT)
    inv = np.float32(10000.0) ** (-np.arange(16, dtype=np.float32) / np.float32(16))
    row, col = (n // 64).astype(np.float32), (n % 64).astype(np.float32)
    ang = np.concatenate([row[:, None] * inv, col[:, None] * inv], axis=1)
    cos, sin = np.cos(ang).T, np.sin(ang).T
    rope = np.concatenate([np.tile(cos, (4, 1)), np.concatenate([-sin, sin, -sin, sin])], axis=1)
    return cst, lvl, rope.astype(np.float32)


def build(nc, A):
    ctx = ExitStack()
    with ctx:
        top = [16512]
        nc_off = {}

        def at(name, shape, dt=F32, where=None):
            size = int(np.prod(shape[1:])) * 4
            if where is None:
                where = top[0]
                top[0] += (size + 31) // 32 * 32
            nc_off[name] = where
            t = nc.alloc_sbuf_tensor_at(name, shape, dt, offset=where)
            return t

        def sem(name):
            return ctx.enter_context(nc.semaphore(name))

        cst = at("cst", [P, 6, P])
        ident, ones = cst[:, 0, :], cst[:, 1, :]
        CUM = (cst[:, 2, :], cst[:, 3, :])
        STRICT = (cst[:, 4, :], cst[:, 5, :])
        xT = at("xT", [P, KC, TOK])
        region_r = top[0]
        raw = [at(f"raw{i}", [P, KC, 2 * P]) for i in range(2)]
        whi = [at(f"whi{i}", [P, KC, P], F32R) for i in range(2)]
        wlo = [at(f"wlo{i}", [P, KC, P], F32R) for i in range(2)]
        vecT = at("vecT", [P, 3, P])
        mods = at("mods", [P, 2, 48, 2])
        wmod = at("wmod", [P, 4, KC, 2])
        allsc = at("allsc", [P, 5, NT, 16])
        gates = at("gates", [P, NT, 32])
        gtmp = at("gtmp", [P, 4, NT, 16])
        gdec = at("gdec", [P, NT, 16])
        sc32 = at("sc32", [P, 4, 16])
        cT = at("cT", [P, KC, 2])
        eps, one = at("eps", [P, 1]), at("one", [P, 1])
        region_h = top[0]
        hh = at("hh", [P, KC, TOK], F32R)
        hl = at("hl", [P, KC, TOK], F32R)
        region_s = top[0]
        rstd = at("rstd", [P, TOK])
        xn = at("xn", [P, 2, TOK])
        top[0] = region_s + 12416
        adaw = [at(f"adaw{i}", [P, KC, P]) for i in range(2)]
        region_q = top[0]
        qkv = at("qkv", [P, 24, SLOT])
        assert top[0] <= 229344, top[0]
        xr = at("xr", [P, 2, SLOT + 4], where=region_s)
        cv = at("cv", [P, 2, SLOT], where=region_s + 6208)
        zst = at("zst", [P, 2, TOK], where=region_s)
        xin = at("xin", [P, NT, D], where=region_q)
        sqb = at("sqb", [P, KC, TOK], where=region_q + 24576)
        vecR = at("vecR", [P, 3, P], where=region_q + 49152)
        wgr = at("wgr", [P, KC, 32], where=region_q + 64000)
        wgh = at("wgh", [P, KC, 32], F32R, where=region_q + 65024)
        wgl = at("wgl", [P, KC, 32], F32R, where=region_q + 66048)
        top[0] = region_h
        lvl = at("lvl", [P, 2, LEVELS, P])
        TU = at("TU", [P, 3, NM, P])
        Pm = at("Pm", [P, NM, P])
        vS = at("vS", [P, SLOT])
        rr = [at(f"rr{d}", [P, P]) for d in range(2)]
        nu = [at(f"nu{d}", [P, P]) for d in range(2)]
        nuk = [at(f"nuk{d}", [P, P]) for d in range(2)]
        Am, QKT, qd, kN, vN, qS, kS, l2b = [], [], [], [], [], [], [], []
        for i in (1, 0):
            if i == 0:
                assert top[0] <= region_q, (top[0], region_q)
                top[0] = region_r
            Am.insert(0, at(f"Am{i}", [P, NM, P]))
            qd.insert(0, at(f"qd{i}", [P, NM, P]))
            QKT.insert(0, at(f"QKT{i}", [P, NM, P]))
            kN.insert(0, at(f"kN{i}", [P, NT, P]))
            vN.insert(0, at(f"vN{i}", [P, NT, P]))
            qS.insert(0, at(f"qS{i}", [P, SLOT]))
            kS.insert(0, at(f"kS{i}", [P, SLOT]))
            l2b.insert(0, at(f"l2b{i}", [P, 2, SLOT], where=nc_off[f"Am{i}"]))
        SC = [at(f"SC{i}", [P, 5, 2, NT]) for i in range(2)]
        St = [at(f"S{d}", [P, P]) for d in range(2)]
        assert top[0] <= region_r + 32768, top[0]
        OB = vS
        zin = at("zin", [P, HEADS, TOK], where=region_q + 16 * 4 * SLOT)
        hidh = at("hidh", [P, KC, TOK], F32R, where=region_q)
        hidl = at("hidl", [P, KC, TOK], F32R, where=region_q + 24576)
        mtmp = at("mtmp", [P, 2, TOK], where=region_q + 49152)
        msq = at("msq", [P, 2, TOK], where=region_q + 55296)
        qT = at("qT", [P, HEADS, LAT], where=region_q)
        kT = at("kT", [P, HEADS, TOK], where=region_q + 16384)
        vT = at("vT", [P, HEADS, TOK], where=region_q + 40960)
        ropt = at("ropt", [P, 2, LAT], where=region_s)
        rsw = at("rsw", [P, 2, LAT], where=region_s + 4096)
        rcs = at("rcs", [P, LAT], where=region_s + 8192)
        lamb = at("lamb", [P, 2, 2, 64], where=region_s + 10240)
        atop = region_h
        qz = at("qz", [P, 2, LAT], where=atop)
        vn = at("vn", [P, NT, P], where=atop + 4096)
        pr = at("pr", [P, 2, 2, TOK], where=atop + 7168)
        pc = at("pc", [P, 2, TOK], where=atop + 19456)
        pT = at("pT", [P, NT, LAT], where=atop + 25600)
        ast = at("ast", [P, 8, 8], where=atop + 37888)
        vs2 = at("vs2", [P, TOK], where=atop + 38400)
        osq = at("osq", [P, 2, LAT], where=atop + 41472)
        orr = at("orr", [P, LAT], where=atop + 45568)
        fin = at("fin", [P, 4, D], where=region_q + 49152)

        bank = ctx.enter_context(nc.psum_tensor("bank", [P, 8, 512], F32))
        pb = [bank[:, i, :] for i in range(8)]
        sps = [bank[:, 2 + 2 * m:4 + 2 * m, :] for m in range(2)]
        zdram = nc.dram_tensor("z_scratch", [HEADS, P, TOK], F32, kind="Internal").ap()

        s_cst, s_x, s_vec, s_wg = sem("s_cst"), sem("s_x"), sem("s_vec"), sem("s_wg")
        s_raw = [sem(f"s_raw{i}") for i in range(2)]
        s_ada = [sem(f"s_ada{i}") for i in range(2)]
        hi_done, lo_done, proj_done, drained = sem("hi_done"), sem("lo_done"), sem("proj_done"), sem("drained")
        ada_done = sem("ada_done")
        xin_t = sem("xin_t")
        vec_t, vec_ready, c_ready = sem("vec_t"), sem("vec_ready"), sem("c_ready")
        mod_ready = sem("mod_ready")
        sq_ready, ss_ready, sd_ready, rs_ready = sem("sq_ready"), sem("ss_ready"), sem("sd_ready"), sem("rs_ready")
        xn_ready, hm_ready, hh_ready, hl_ready = sem("xn_ready"), sem("hm_ready"), sem("hh_ready"), sem("hl_ready")
        pads, wg_hi, wg_lo, gate_ps = sem("pads"), sem("wg_hi"), sem("wg_lo"), sem("gate_ps")
        kon, a_mods = sem("kon"), sem("a_mods")
        sc_all, xT_lat, xT_ctx = sem("sc_all"), sem("xT_lat"), sem("xT_ctx")
        o_sum = [sem(f"o_sum{d}") for d in range(2)]
        ga, gv, gp = sem("ga"), sem("gv"), sem("gp")
        xr_ready, conv_step, silu_done, z_ready, zs = sem("xr_ready"), sem("conv_step"), sem("silu_done"), sem("z_ready"), [sem(f"z_stored{i}") for i in range(2)]
        sq_done, hid_hi, hid_lo = sem("sq_done"), sem("hid_hi"), sem("hid_lo")
        s_lvl, s_zin = sem("s_lvl"), sem("s_zin")
        l2_sq, l2_ss, l2_sd, l2_rc, qk_ready = sem("l2_sq"), sem("l2_ss"), sem("l2_sd"), sem("l2_rc"), sem("qk_ready")
        sc_ready, gu_ready, grow_ps, eg_ready = sem("sc_ready"), sem("gu_ready"), sem("grow_ps"), sem("eg_ready")
        x_ready, xm_ready, dec_ready, qd_ready = sem("x_ready"), sem("xm_ready"), sem("dec_ready"), sem("qd_ready")
        vs_ready, kv_t, kv_nat, kk_ps, qk_ps = sem("vs_ready"), sem("kv_t"), sem("kv_nat"), sem("kk_ps"), sem("qk_ps")
        am_step, qkt_step, t_pair, tu_init = sem("am_step"), sem("qkt_step"), sem("t_pair"), sem("tu_init")
        qkt_mask = sem("qkt_mask")
        p_ps, p_ready, x_ps, tu_ready, ub_ready = sem("p_ps"), sem("p_ready"), sem("x_ps"), sem("tu_ready"), sem("ub_ready")
        ks_ps = [sem(f"ks_ps{d}") for d in range(2)]
        r_ready = [sem(f"r_ready{d}") for d in range(2)]
        nu_ps = [sem(f"nu_ps{d}") for d in range(2)]
        nu_ready = [sem(f"nu_ready{d}") for d in range(2)]
        o_ps = [sem(f"o_ps{d}") for d in range(2)]
        ds_ps = [sem(f"ds_ps{d}") for d in range(2)]
        s_new = [sem(f"s_new{d}") for d in range(2)]
        head_out = sem("head_out")
        f_sq, f_ss, f_sd, f_rc, f_y1, f_y = sem("f_sq"), sem("f_ss"), sem("f_sd"), sem("f_rc"), sem("f_y1"), sem("f_y")
        y_hi, y_lo = sem("y_hi"), sem("y_lo")
        s_rope, rp_sw, rp_cos, rp_sin = sem("s_rope"), sem("rp_sw"), sem("rp_cos"), sem("rp_sin")
        lam_a, lam_v = sem("lam_a"), sem("lam_v")
        qz_zero, qz_ready, vt_ps, vn_ready = sem("qz_zero"), sem("qz_ready"), sem("vt_ps"), sem("vn_ready")
        s_ps, mx_ready, nm_ready, e_ready, rl_ready = sem("s_ps"), sem("mx_ready"), sem("nm_ready"), sem("e_ready"), sem("rl_ready")
        p0_ready, pc_ready, pt_ps, pT_ready, at_ps = sem("p0_ready"), sem("pc_ready"), sem("pt_ps"), sem("pT_ready"), sem("at_ps")
        a_sq, a_ss, a_sd, a_rc, a_y = sem("a_sq"), sem("a_ss"), sem("a_sd"), sem("a_rc"), sem("a_y")
        fin_n, fin_ps, fin_ready, s_out = sem("fin_n"), sem("fin_ps"), sem("fin_ready"), sem("s_out")

        block = ctx.enter_context(nc.Block())

        def ds(i, n=1):
            return slice(i, i + n) if isinstance(i, int) else bass.ds(i, n)

        def row(t, i):
            return t[:, ds(i), :].rearrange("p a n -> p (a n)")

        def bc(ap, n):
            return ap.unsqueeze(2).broadcast_to([P, ap.shape[1], n])

        def over(ap, n):
            return ap.unsqueeze(1).broadcast_to([P, n, ap.shape[1]])

        def chunks(t, c0, n):
            return t[:, off(c0):off(c0) + n * P].rearrange("p (c i) -> p c i", i=P)

        def kview(w):
            return w.rearrange("(k p) n -> p k n", p=P)

        def tu_ap(g, level, par):
            s, d = 1 << level, g // 2
            u = (1 + par) * NM * P
            par_t, par_u = (0, 1) if d == 0 else (1, 0)
            return bass.AP(TU[:, 0, 0, :].tensor, 3 * g * P + par_t * s,
                           [[3 * NM * P, P], [u + (par_u - par_t) * s, 2], [2 * s, 3 * P // (2 * s)], [1, s]])

        def half(ap, s, par):
            return ap.rearrange("p (b two c) -> p b two c", two=2, c=s)[:, :, par, :]

        norm_tokens = {0: GROUPS, 1: GROUPS, 2: GROUPS, 3: GROUPS[:1], 4: GROUPS[:1]}

        def gate(layer, part, o, v):
            return mods[:, layer, part * KC + o, v:v + 1]

        @block.sync
        def _(sp):
            sp.dma_start(cst[:, :, :], A["cst"].rearrange("p (a n) -> p a n", a=6)).then_inc(s_cst, 16)
            sp.dma_start(vecR[0:48, 0, :], A["ada_b"][0].rearrange("(r n) -> r n", n=P)).then_inc(s_vec, 16)
            sp.dma_start(vecR[48:96, 0, :], A["ada_b"][1].rearrange("(r n) -> r n", n=P)).then_inc(s_vec, 16)
            sp.dma_start(vecR[96:128, 0, :], A["norm_w"].rearrange("i j (r n) -> (i j r) n", n=P)).then_inc(s_vec, 16)
            sp.dma_start(vecR[0:120, 1, :], A["dn_conv"][0].rearrange("w (r n) -> (w r) n", n=P)).then_inc(s_vec, 16)
            sp.dma_start(vecR[120:128, 1, :], A["final_norm"].rearrange("(r n) -> r n", n=P)).then_inc(s_vec, 16)
            sp.dma_start(vecR[0:8, 2, :], A["c"][0].rearrange("(r n) -> r n", n=P)).then_inc(s_vec, 16)
            sp.dma_start(vecR[8:16, 2, :], A["c_ctx"].rearrange("(r n) -> r n", n=P)).then_inc(s_vec, 16)
            sp.dma_start(vecR[16:17, 2, :], A["dn_out_norm"]).then_inc(s_vec, 16)
            sp.dma_start(vecR[17:18, 2, :], A["da_subln"]).then_inc(s_vec, 16)
            sp.dma_start(xin[:, 0:2, :], A["ctx"][0].rearrange("(t p) d -> p t d", p=P)).then_inc(s_x, 16)
            sp.dma_start(xin[:, 2:6, :], A["x"][0].rearrange("(t p) d -> p t d", p=P)).then_inc(s_x, 16)

            def load_ada(layer, a, slot, tile, free=None):
                if free is not None:
                    sp.wait_ge(ada_done, free)
                sp.dma_start(adaw[slot][:, :, :], kview(A["ada_w"][layer])[:, :, ds(tile * P, P)]).then_inc(s_ada[slot], 16)

            def load_w(g, slot, src, first=False):
                if not first:
                    sp.wait_ge(lo_done, 2 * g - 2)
                sp.dma_start(raw[slot][:, :, :], src).then_inc(s_raw[slot], 16)

            w_in = kview(A["dn_w_in"][0])
            load_ada(0, 0, 0, 0)
            load_ada(0, 1, 1, 1)
            sp.dma_start(wgr[:, :, :], w_in[:, :, 4096:4128]).then_inc(s_wg, 16)
            sp.dma_start(sc32[:, 0, :], A["dn_a_log"].rearrange("a d h -> a (d h)").broadcast_to([P, 16])).then_inc(s_wg, 16)
            sp.dma_start(sc32[:, 1, :], A["dn_dt_bias"].rearrange("a d h -> a (d h)").broadcast_to([P, 16])).then_inc(s_wg, 16)
            for j in range(2):
                load_w(j, j, w_in[:, :, 256 * j:256 * (j + 1)], first=True)
            with sp.Fori(1, 8) as i:
                for j in range(2):
                    load_ada(0, 2 * i + j, j, 2 * i + j, free=2 * i + j - 1)

            def dnin_loads(b, skip=False):
                for j in range(2):
                    if not skip:
                        load_w(2 * b + j, j, w_in[:, :, ds((2 * b + j) * 256, 256)])
                    for v in range(2):
                        tile = 16 + 4 * b + 2 * j + v
                        load_ada(0, tile, v, tile, free=tile - 1)

            dnin_loads(0, skip=True)
            with sp.Fori(1, 8) as b:
                dnin_loads(b)
            sp.wait_ge(proj_done, S_DNOUT)
            sp.dma_start(lvl[:, :, :, :], A["lvl"].rearrange("p (d l n) -> p d l n", d=2, l=LEVELS)).then_inc(s_lvl, 16)
            w_out = kview(A["dn_w_out"][0])
            g0 = S_DNOUT // 2
            sp.wait_ge(head_out, HEADS)
            sp.wait_ge(tu_init, HEADS)
            for j in range(4):
                load_w(g0 + j, j % 2, w_out[:, :, 256 * j:256 * (j + 1)])
                if j == 1:
                    sp.dma_start(zin[:, :, :], zdram.rearrange("h p n -> p h n")).then_inc(s_zin, 16)

            def mlp_loads(layer, blk, g0):
                w1, w2 = kview(A["mlp_w1"][layer]), kview(A["mlp_w2"][layer])
                for j in range(8):
                    if j < 4:
                        src = w1[:, :, ds(blk * 1024 + 256 * j, 256)]
                    else:
                        src = w2[:, ds(blk * 8, 8), 256 * (j - 4):256 * (j - 3)]
                    load_w(g0 + 8 * blk + j, j % 2, src)
                    if layer == 0 and j < 6:
                        for v in range(2):
                            tile = 12 * blk + 2 * j + v
                            load_ada(1, tile, v, tile, free=48 + tile - 1)

            with sp.Fori(0, 4) as blk:
                mlp_loads(0, blk, S_MLP0 // 2)
            w_qkv, g0 = kview(A["da_w_qkv"][0]), S_QKV // 2

            def qkv_loads(b):
                for j in range(2):
                    load_w(g0 + 2 * b + j, j, w_qkv[:, :, ds((2 * b + j) * 256, 256)])

            qkv_loads(0)
            sp.wait_ge(hl_ready, 24)
            sp.dma_start(ropt[:, :, :], A["rope"].rearrange("p (a n) -> p a n", a=2)).then_inc(s_rope, 16)
            sp.dma_start(lamb[:, :, :, :].rearrange("p a b n -> p (a b n)"),
                         A["da_lambda"].rearrange("a r n -> a (r n)").broadcast_to([P, 256])).then_inc(s_rope, 16)
            with sp.Fori(1, 6) as b:
                qkv_loads(b)
            w_out2, g0 = kview(A["da_w_out"][0]), S_DAOUT // 2
            for j in range(4):
                load_w(g0 + j, j % 2, w_out2[:, :, 256 * j:256 * (j + 1)])
            with sp.Fori(0, 4) as blk:
                mlp_loads(1, blk, S_MLP1 // 2)
            for t in range(4):
                sp.wait_ge(fin_ready, 2 * t + 2)
                sp.dma_start(A["out"][0, t * P:(t + 1) * P, :], fin[:, t, :]).then_inc(s_out, 16)
            sp.wait_ge(s_out, 64)

        @block.gpsimd
        def _(pool):
            pool.memset(eps[:, :], EPS)
            pool.memset(one[:, :], 1.0).then_inc(kon, 1)
            pool.wait_ge(hl_ready, 8)
            for t in range(2):
                pool.memset(xr[:, t, 0:2], 0.0)
                pool.memset(xr[:, t, 258:262], 0.0)
                pool.memset(xr[:, t, 774:776], 0.0).then_inc(pads, 1)
            for h in range(HEADS):
                pool.wait_ge(drained, 24 + h + 1)
                pool.dma_start(zdram[h], zst[:, h % 2, :]).then_inc(zs[h % 2], 16)
            pool.wait_ge(zs[0], 64)
            pool.wait_ge(zs[1], 64)

            def head_rows(n, q):
                pool.tensor_copy(vS[:, 0:SLOT], row(qkv, 16 + n)).then_inc(vs_ready, 1)
                for k in range(5):
                    i = pool.tensor_copy(SC[q][:, k, :, :],
                                         allsc[:, k, :, :].rearrange("p c (d h) -> p d c h", d=2)[:, :, :, ds(n)].rearrange("p d c h -> p d (c h)"))
                i.then_inc(sc_ready, 1)
                for d in range(2):
                    g = gdec[:, :, ds(n + 8 * d)].rearrange("p c h -> p (c h)")
                    pool.tensor_tensor(QKT[q][:, d * NT:(d + 1) * NT, :], over(CUM[d], NT), bc(g, P), ALU.mult).then_inc(gu_ready, 1)

            def triangles(n, q):
                pool.wait_ge(qkt_step, 4 * n + 4)
                for d in range(2):
                    m = pool.tensor_tensor(QKT[q][:, NT * d:NT * (d + 1), :], QKT[q][:, NT * d:NT * (d + 1), :], over(CUM[d], NT), ALU.mult)
                m.then_inc(qkt_mask, 1)

            def first_t(n, q):
                pool.wait_ge(am_step, 5 * n + 5)
                for d in range(2):
                    m = pool.tensor_tensor(TU[:, 0, NT * d:NT * (d + 1), :], Am[q][:, NT * d:NT * (d + 1), :], over(lvl[:, 1 - d, 0, :], NT), ALU.mult)
                m.then_inc(t_pair, 1)
                pool.wait_ge(t_pair, n + 1)
                pool.tensor_tensor(TU[:, 0, :, :], over(ident, NM), TU[:, 0, :, :], ALU.subtract).then_inc(tu_init, 1)

            pool.wait_ge(silu_done, 24)
            pool.wait_ge(sc_all, 1)
            pool.wait_ge(proj_done, S_DNOUT)
            head_rows(0, 0)
            triangles(0, 0)
            pool.wait_ge(s_lvl, 16)
            first_t(0, 0)

            def pair(i, last=False):
                for q in range(2):
                    n = 2 * i + q
                    if last and q:
                        break
                    pool.wait_ge(head_out, 1 + n)
                    pool.wait_ge(kv_t, n + 1)
                    head_rows(n + 1, 1 - q)
                    triangles(n + 1, 1 - q)
                    pool.wait_ge(tu_ready, 28 * n + 28)
                    first_t(n + 1, 1 - q)

            with pool.Fori(0, 3) as i:
                pair(i)
            pair(3, last=True)

        @block.scalar
        def _(act):
            def split(s, slot, par, nth):
                act.wait_ge(s_raw[slot], nth)
                if not isinstance(s, int) or s >= 2:
                    act.wait_ge(proj_done, s - 1)
                act.activation(whi[par][:, :, :], raw[slot][:, :, par * P:(par + 1) * P], ACT.Copy).then_inc(hi_done, 1)

            def split_next(s, u):
                v = u + 1
                g = (s + 1 - (v % 2)) // 2 if isinstance(s, int) else None
                slot = (v // 2) % 2
                split(s + 1, slot, v % 2, (s - u) * 4 + 16 * (v // 4 + 1))

            def norm(nu_, pre=None):
                base = 8 * nu_
                groups = norm_tokens[nu_]
                for k in range(KC):
                    if nu_ == 0:
                        act.wait_ge(xT_lat, k + 1)
                        act.wait_ge(xT_ctx, k + 1)
                    elif k == 0:
                        act.wait_ge(drained, pre)
                    t0 = groups[-1][0].start
                    act.activation(sqb[:, k, t0:TOK], xT[:, k, t0:TOK], ACT.Square).then_inc(sq_ready, 1)
                act.wait_ge(ss_ready, nu_ + 1)
                for i, (cols, n, v) in enumerate(groups):
                    ins = act.activation(rstd[:, cols], pb[4 + i][:, 0:n], ACT.Ln, scale=1.0 / D, bias=eps[:, 0:1])
                ins.then_inc(sd_ready, 1)
                act.wait_ge(sd_ready, nu_ + 1)
                t0 = groups[-1][0].start
                act.activation(rstd[:, t0:TOK], rstd[:, t0:TOK], ACT.Exp, scale=-0.5).then_inc(rs_ready, 1)
                if nu_ == 4:
                    return
                layer, part = nu_ // 2, 3 * (nu_ % 2)
                for k in range(KC):
                    act.wait_ge(xn_ready, base + k + 1)
                    for cols, n, v in groups:
                        ins = act.activation(xn[:, k % 2, cols], xn[:, k % 2, cols], ACT.Identity,
                                             scale=wmod[:, nu_, k, v:v + 1], bias=gate(layer, part, k, v))
                    ins.then_inc(hm_ready, 1)
                    act.wait_ge(hm_ready, base + k + 1)
                    t0 = groups[-1][0].start
                    act.activation(hh[:, k, t0:TOK], xn[:, k % 2, t0:TOK], ACT.Copy).then_inc(hh_ready, 1)

            act.wait_ge(kon, 1)
            act.wait_ge(vec_ready, 2)
            act.activation(cT[:, :, :], vecT[:, 2, 0:16].rearrange("p (v k) -> p k v", v=2), ACT.Silu).then_inc(c_ready, 1)
            for k in range(KC):
                act.wait_ge(xin_t, k + 1)
                act.activation(xT[:, k, LATS], pb[2 * (k % 2)][:, :], ACT.Copy).then_inc(xT_lat, 1)
            split(0, 0, 0, 16)
            act.wait_ge(s_wg, 48)
            act.activation(wgh[:, :, :], wgr[:, :, :], ACT.Copy).then_inc(wg_hi, 1)
            norm(0)
            act.wait_ge(gv, 3)
            act.activation(gtmp[:, 2, :, :], gtmp[:, 1, :, :], ACT.Exp, scale=-1.0).then_inc(ga, 1)
            act.activation(sc32[:, 2, :], sc32[:, 0, :], ACT.Exp).then_inc(ga, 1)
            act.activation(gtmp[:, 3, :, :], gates[:, :, 16:32], ACT.Exp, scale=-1.0).then_inc(ga, 1)
            act.wait_ge(ga, 1)
            act.activation(gtmp[:, 2, :, :], gtmp[:, 2, :, :], ACT.Ln, bias=one[:, 0:1]).then_inc(ga, 1)
            act.wait_ge(gv, 10)
            act.activation(allsc[:, 1, :, :], allsc[:, 0, :, :], ACT.Exp).then_inc(ga, 1)
            act.activation(allsc[:, 2, :, :], gtmp[:, 0, :, :], ACT.Exp).then_inc(ga, 1)
            act.activation(allsc[:, 3, :, :].rearrange("p a b -> p (a b)"), pb[7][:, 96:192], ACT.Exp).then_inc(ga, 1)

            def silu_row(s, par):
                act.wait_ge(conv_step, 5 * s + 5)
                act.activation(row(qkv, s), cv[:, par, :], ACT.Silu).then_inc(silu_done, 1)

            def dnin(b, first=False, z=False):
                for u in range(4):
                    s = 4 * b + u
                    if not (z and s == S_DNOUT - 1):
                        split_next(s, u)
                    if not (first and u == 0) and not (z and s > 24):
                        silu_row(s - 1, (u + 1) % 2)
                    act.wait_ge(proj_done, s + 1)
                    if z:
                        if s >= 26:
                            act.wait_ge(zs[u % 2], 16 * ((s - 24) // 2))
                        act.activation(zst[:, u % 2, CTXS], pb[2 * (u % 2) + 1][:, 0:CTX], ACT.Silu)
                        act.activation(zst[:, u % 2, LATS], pb[2 * (u % 2)][:, :], ACT.Silu).then_inc(drained, 1)
                        continue
                    if not first or u >= 2:
                        act.wait_ge(conv_step, 5 * (s - 1))
                    else:
                        act.wait_ge(pads, 2)
                    act.activation(xr[:, u % 2, 2:258], pb[2 * (u % 2) + 1][:, 0:CTX], ACT.Copy)
                    act.activation(xr[:, u % 2, 262:774], pb[2 * (u % 2)][:, :], ACT.Copy).then_inc(drained, 1)

            dnin(0, first=True)
            with act.Fori(1, 6) as b:
                dnin(b)
            dnin(6, z=True)
            dnin(7, z=True)

            def prepare(n, q):
                act.wait_ge(vs_ready, n + 1)
                act.activation(l2b[q][:, 0, :], row(qkv, n), ACT.Square)
                act.activation(l2b[q][:, 1, :], row(qkv, 8 + n), ACT.Square).then_inc(l2_sq, 1)
                act.wait_ge(l2_ss, n + 1)
                for i in range(4):
                    ins = act.activation(l2b[q][:, i // 2, (i % 2) * 386:(i % 2 + 1) * 386], pb[4 + i][:, 0:386], ACT.Ln, bias=eps[:, 0:1])
                ins.then_inc(l2_sd, 1)
                act.wait_ge(l2_sd, n + 1)
                act.activation(l2b[q][:, :, :], l2b[q][:, :, :], ACT.Exp, scale=-0.5).then_inc(l2_rc, 1)
                act.wait_ge(qk_ready, 2 * n + 2)
                for g in range(4):
                    act.wait_ge(x_ready, 4 * n + g + 1)
                    act.activation(qd[q][:, 3 * g:3 * g + 3, :].rearrange("p c i -> p (c i)"), pb[4 + g][:, 0:384], ACT.Exp).then_inc(eg_ready, 1)
                act.wait_ge(xm_ready, 2 * n + 1)
                act.activation(QKT[q][:, :, :], QKT[q][:, :, :], ACT.Exp).then_inc(dec_ready, 1)
                act.wait_ge(xm_ready, 2 * n + 2)
                act.activation(Am[q][:, :, :], Am[q][:, :, :], ACT.Exp, scale=-1.0).then_inc(dec_ready, 1)
                act.wait_ge(kv_t, n + 1)
                for i in range(4):
                    dst = (kN, vN)[i // 2][q][:, 3 * (i % 2):3 * (i % 2) + 3, :]
                    ins = act.activation(dst.rearrange("p c i -> p (c i)"), pb[4 + i][:, 0:384], ACT.Copy)
                ins.then_inc(kv_nat, 1)

            def recur(n, q):
                def beta_rows(g):
                    act.wait_ge(tu_ready, 28 * n + 24 + g + 1)
                    for m in range(3 * g, 3 * g + 3):
                        ins = act.activation(TU[:, 1 + q, m, :], TU[:, 1 + q, m, :], ACT.Copy, scale=SC[q][:, 4, m // NT, m % NT:m % NT + 1])
                    ins.then_inc(ub_ready, 1)

                beta_rows(0)
                beta_rows(2)
                for t in range(NT):
                    for d in range(2):
                        c = ORDER[d][t]
                        act.wait_ge(nu_ps[d], NT * n + t + 1)
                        act.activation(nuk[d][:, :], pb[4 * d + 1][:, 0:P], ACT.Copy, scale=SC[q][:, 2, d, c:c + 1]).then_inc(nu_ready[d], 1)
                        act.activation(nu[d][:, :], pb[4 * d + 1][:, 0:P], ACT.Copy).then_inc(nu_ready[d], 1)
                    if t < 2:
                        beta_rows((3, 1)[t])

            prepare(0, 0)

            def pair(i, last=False):
                prepare(2 * i + 1, 1)
                recur(2 * i, 0)
                if not last:
                    prepare(2 * i + 2, 0)
                recur(2 * i + 1, 1)

            with act.Fori(0, 3) as i:
                pair(i)
            pair(3, last=True)

            for h in range(HEADS):
                if h == 0:
                    act.wait_ge(head_out, 1 + HEADS)
                act.activation(qkv[:, 8 + h, 0:TOK], qkv[:, h, 0:TOK], ACT.Square).then_inc(f_sq, 1)
            split(S_DNOUT, 0, 0, 4 * S_DNOUT + 16)
            for h in range(HEADS):
                act.wait_ge(f_ss, h + 1)
                for i in range(2):
                    ins = act.activation(qkv[:, 8 + h, 384 * i:384 * (i + 1)], pb[2 * (h % 4) + i][:, 0:384], ACT.Ln, scale=1.0 / P, bias=eps[:, 0:1])
                ins.then_inc(f_sd, 1)
                act.wait_ge(f_sd, h + 1)
                act.activation(qkv[:, 8 + h, 0:TOK], qkv[:, 8 + h, 0:TOK], ACT.Exp, scale=-0.5).then_inc(f_rc, 1)
            for h in range(HEADS):
                act.wait_ge(f_y, h + 1)
                act.activation(hh[:, h, :], qkv[:, h, 0:TOK], ACT.Copy).then_inc(y_hi, 1)

            for u in range(8):
                split_next(S_DNOUT + u, u % 4)
            norm(1, pre=S_MLP0)

            def mlp(layer, blk, last=False):
                groups = norm_tokens[1 + 2 * layer]
                t0 = groups[-1][0].start
                base = (S_MLP0, S_MLP1)[layer]
                for u in range(16):
                    s = base + 16 * blk + u
                    if not (last and u == 15):
                        split_next(s, u % 4)
                    if u < 8:
                        m = 32 * layer + 8 * blk + u
                        act.wait_ge(proj_done, s + 1)
                        if not (isinstance(m, int) and m < 2):
                            act.wait_ge(sq_done, m - 1)
                            act.wait_ge(hid_hi, m - 1)
                        for i, (cols, n, v) in enumerate(groups):
                            ins = act.activation(mtmp[:, u % 2, cols], pb[2 * (u % 2) + i][:, 0:n], ACT.Relu)
                        ins.then_inc(drained, 1)
                        act.wait_ge(drained, s + 1)
                        act.activation(hidh[:, u, t0:TOK], mtmp[:, u % 2, t0:TOK], ACT.Square).then_inc(hid_hi, 1)

            mlp(0, 0)
            with act.Fori(1, 4) as blk:
                mlp(0, blk)
            norm(2, pre=S_QKV)

            def qkvs(b, kind):
                for u in range(4):
                    s = S_QKV + 4 * b + u
                    split_next(s, u)
                    act.wait_ge(proj_done, s + 1)
                    lat = pb[2 * (u % 2)]
                    o = 4 * b + u
                    if kind == 2:
                        act.activation(row(vT, o - 16)[:, CTXS], pb[2 * (u % 2) + 1][:, 0:CTX], ACT.Copy)
                        act.activation(row(vT, o - 16)[:, LATS], lat[:, :], ACT.Copy).then_inc(drained, 1)
                        continue
                    if kind == 1:
                        act.activation(row(kT, o - 8)[:, CTXS], pb[2 * (u % 2) + 1][:, 0:CTX], ACT.Copy)
                        act.activation(row(kT, o - 8)[:, LATS], lat[:, :], ACT.Copy)
                    else:
                        act.activation(row(qT, o), lat[:, :], ACT.Copy)
                    if not (isinstance(o, int) and o < 2):
                        act.wait_ge(rp_sin, o - 1)
                    for q in range(4):
                        ins = act.activation(rsw[32 * q:32 * q + 32, u % 2, :], lat[32 * (q ^ 1):32 * (q ^ 1) + 32, :], ACT.Copy)
                    ins.then_inc(drained, 1)

            for b in range(6):
                qkvs(b, b // 2)

            act.wait_ge(lam_v, 2)
            act.activation(sc32[:, 3, 2:4], sc32[:, 3, 0:2], ACT.Exp).then_inc(lam_a, 1)

            def attend(h, first=False):
                if first:
                    act.wait_ge(qz_zero, 1)
                    act.wait_ge(drained, S_DAOUT)
                    act.wait_ge(rp_sin, 16)
                else:
                    act.wait_ge(s_ps, 8 * h)
                    act.wait_ge(vt_ps, h)
                act.activation(qz[0:64, 0, :], row(qT, h)[0:64, :], ACT.Copy)
                act.activation(qz[64:P, 1, :], row(qT, h)[64:P, :], ACT.Copy)
                act.activation(vs2[:, :], row(vT, h), ACT.Copy).then_inc(qz_ready, 1)
                act.wait_ge(vt_ps, h + 1)
                if not first:
                    act.wait_ge(at_ps, h)
                for i in range(2):
                    ins = act.activation(vn[:, 3 * i:3 * i + 3, :].rearrange("p c i -> p (c i)"), pb[i][:, 0:384], ACT.Copy)
                ins.then_inc(vn_ready, 1)
                for t in range(4):
                    for m in range(2):
                        e = 2 * t + m
                        act.wait_ge(nm_ready, 8 * h + e + 1)
                        if not (first and t < 2):
                            act.wait_ge(pc_ready, 4 * h + t - 1)
                        act.activation(pr[:, t % 2, m, :].rearrange("p (a k) -> p a k", a=2), sps[m][:, :, 0:384], ACT.Exp,
                                       scale=0.125, bias=ast[:, 2 + m, t:t + 1],
                                       accum_out=ast[:, 4 + m, t:t + 1]).then_inc(e_ready, 1)
                act.wait_ge(at_ps, h + 1)
                act.activation(osq[:, 0, :], pb[6][:, :], ACT.Square)
                act.activation(osq[:, 1, :], pb[6][:, :], ACT.Copy).then_inc(a_sq, 1)
                act.wait_ge(a_ss, h + 1)
                act.activation(orr[:, :], pb[7][:, :], ACT.Ln, scale=1.0 / P, bias=eps[:, 0:1]).then_inc(a_sd, 1)
                act.wait_ge(a_sd, h + 1)
                act.activation(orr[:, :], orr[:, :], ACT.Exp, scale=-0.5).then_inc(a_rc, 1)

            attend(0, first=True)
            with act.Fori(1, HEADS) as h:
                attend(h)
            for h in range(HEADS):
                if h == 0:
                    act.wait_ge(a_y, HEADS)
                act.activation(hh[:, h, LATS], qT[:, h, :], ACT.Copy).then_inc(y_hi, 1)
            for u in range(8):
                split_next(S_DAOUT + u, u % 4)
            norm(3, pre=S_MLP1)
            mlp(1, 0)
            with act.Fori(1, 3) as blk:
                mlp(1, blk)
            mlp(1, 3, last=True)
            norm(4, pre=S_END)
            for t in range(4):
                for i in range(2):
                    act.wait_ge(fin_ps, 2 * t + i + 1)
                    act.activation(fin[:, t, 512 * i:512 * (i + 1)], pb[(2 * t + i) % 4][:, :], ACT.Copy).then_inc(fin_ready, 1)

        @block.vector
        def _(dve):
            def split(s, slot, par):
                dve.wait_ge(hi_done, s + 1)
                dve.tensor_tensor(wlo[par][:, :, :], raw[slot][:, :, par * P:(par + 1) * P], whi[par][:, :, :],
                                  ALU.subtract).then_inc(lo_done, 1)

            def split_next(s, u):
                split(s + 1, ((u + 1) // 2) % 2, (u + 1) % 2)

            def norm(nu_):
                base = 8 * nu_
                groups = norm_tokens[nu_]
                t0 = groups[-1][0].start
                dve.wait_ge(rs_ready, nu_ + 1)
                if nu_ == 4:
                    for k in range(KC):
                        dve.scalar_tensor_tensor(sqb[:, k, LATS], xT[:, k, LATS], vecT[:, 1, 120 + k:121 + k], rstd[:, LATS],
                                                 op0=ALU.mult, op1=ALU.mult).then_inc(fin_n, 1)
                    return

                def low(k):
                    dve.wait_ge(hh_ready, base + k + 1)
                    dve.tensor_tensor(hl[:, k, t0:TOK], xn[:, k % 2, t0:TOK], hh[:, k, t0:TOK], ALU.subtract).then_inc(hl_ready, 1)

                for k in range(KC):
                    if k >= 2:
                        low(k - 2)
                        dve.wait_ge(hl_ready, base + k - 1)
                    dve.tensor_tensor(xn[:, k % 2, t0:TOK], xT[:, k, t0:TOK], rstd[:, t0:TOK], ALU.mult).then_inc(xn_ready, 1)
                low(6)
                low(7)

            chain = [0]

            def link(ins):
                chain[0] += 1
                ins.then_inc(gv, 1)
                dve.wait_ge(gv, chain[0])

            def take_mods(layer, c0, c1, bank_, first_tile, done):
                dve.wait_ge(ada_done, done)
                n = c1 - c0
                src = pb[bank_][:, 2 * c0:2 * c1].rearrange("p (c v) -> p c v", v=2)
                dve.tensor_tensor(mods[:, layer, c0:c1, :], src, bc(vecT[:, 0, 48 * layer + c0:48 * layer + c1], 2), ALU.add).then_inc(mod_ready, 1)

            def take_wmod(i, n_mod):
                layer, part = i // 2, 3 * (i % 2) + 1
                dve.wait_ge(mod_ready, n_mod)
                dve.scalar_tensor_tensor(wmod[:, i, :, :], mods[:, layer, part * KC:(part + 1) * KC, :], 1.0,
                                         bc(vecT[:, 0, 96 + 8 * i:104 + 8 * i], 2), op0=ALU.add, op1=ALU.mult).then_inc(a_mods, 1)
                dve.wait_ge(a_mods, i + 1)

            dve.memset(sc32[:, 3, 8:16], 0.0).then_inc(head_out, 1)
            dve.wait_ge(vec_t, 1)
            dve.tensor_copy(vecT[:, 0:2, :].rearrange("p a n -> p (a n)"), pb[7][:, 0:256])
            dve.tensor_copy(vecT[:, 2, 0:18], pb[7][:, 256:274]).then_inc(vec_ready, 2)
            dve.wait_ge(vec_ready, 2)
            for k in range(KC):
                dve.wait_ge(xin_t, k + 1)
                dve.tensor_copy(xT[:, k, CTXS], pb[2 * (k % 2) + 1][:, 0:CTX]).then_inc(xT_ctx, 1)
            split(0, 0, 0)
            dve.wait_ge(wg_hi, 1)
            dve.tensor_tensor(wgl[:, :, :], wgr[:, :, :], wgh[:, :, :], ALU.subtract).then_inc(wg_lo, 1)
            take_mods(0, 0, 16, 6, 0, 16)
            take_wmod(0, 1)
            norm(0)

            dve.wait_ge(gate_ps, 1)
            link(dve.tensor_copy(gates[:, :, :].rearrange("p a b -> p (a b)"), pb[7][:, 0:192]))
            link(dve.tensor_tensor(gtmp[:, 0, :, :], gates[:, :, 0:16], over(sc32[:, 1, :], NT), ALU.add))
            link(dve.scalar_tensor_tensor(gtmp[:, 1, :, :], gtmp[:, 0, :, :], -1.0, gtmp[:, 0, :, :], op0=ALU.mult, op1=ALU.max))
            dve.wait_ge(ga, 4)
            link(dve.tensor_scalar(gtmp[:, 1, :, :], gtmp[:, 0, :, :], 0.0, None, ALU.max))
            link(dve.tensor_tensor(gtmp[:, 1, :, :], gtmp[:, 1, :, :], gtmp[:, 2, :, :], ALU.add))
            link(dve.scalar_tensor_tensor(gdec[:, :, :], gtmp[:, 1, :, :], -1.0, over(sc32[:, 2, :], NT), op0=ALU.mult, op1=ALU.mult))
            link(dve.tensor_scalar(gtmp[:, 3, :, :], gtmp[:, 3, :, :], 1.0, None, ALU.add))
            link(dve.reciprocal(allsc[:, 4, :, :], gtmp[:, 3, :, :]))
            dve.wait_ge(gp, 1)
            link(dve.tensor_copy(allsc[:, 0, :, :].rearrange("p t (d h) -> p d t h", d=2),
                                 pb[7][:, 0:96].rearrange("p (d t h) -> p d t h", d=2, t=NT)))
            link(dve.tensor_tensor(gtmp[:, 0, :, :].rearrange("p a b -> p (a b)"), pb[7][:, 96:192],
                                   allsc[:, 0, :, :].rearrange("p a b -> p (a b)"), ALU.subtract))
            dve.wait_ge(ga, 7)
            dve.tensor_scalar(allsc[:, 1, :, :], allsc[:, 1, :, :], -1.0, None, ALU.mult).then_inc(sc_all, 1)

            def dnin(b, first=False, z=False):
                for u in range(4):
                    s = 4 * b + u
                    if not (z and s == S_DNOUT - 1):
                        split_next(s, u)
                    if z:
                        continue
                    dve.wait_ge(drained, s + 1)
                    if not first or u >= 2:
                        dve.wait_ge(silu_done, s - 1)
                    dve.tensor_scalar(cv[:, u % 2, :], xr[:, u % 2, 0:SLOT], vecT[:, 1, ds(s)], None, ALU.mult).then_inc(conv_step, 1)
                    for w in range(1, 5):
                        dve.wait_ge(conv_step, 5 * s + w)
                        dve.scalar_tensor_tensor(cv[:, u % 2, :], xr[:, u % 2, w:w + SLOT], vecT[:, 1, ds(24 * w + s)], cv[:, u % 2, :],
                                                 op0=ALU.mult, op1=ALU.add).then_inc(conv_step, 1)

            dnin(0, first=True)
            with dve.Fori(1, 6) as b:
                dnin(b)
            dnin(6, z=True)
            dnin(7, z=True)
            take_mods(0, 16, 48, 6, 16, 48)
            take_wmod(1, 2)

            def unit_length(n, q):
                dve.wait_ge(l2_rc, n + 1)
                dve.scalar_tensor_tensor(qS[q][:, :], l2b[q][:, 0, :], float(P) ** -0.5, row(qkv, n), op0=ALU.mult, op1=ALU.mult).then_inc(qk_ready, 1)
                dve.tensor_tensor(kS[q][:, :], l2b[q][:, 1, :], row(qkv, 8 + n), ALU.mult).then_inc(qk_ready, 1)

            def exponents(n, q):
                dve.wait_ge(sc_ready, n + 1)
                dve.wait_ge(qk_ready, 2 * n + 2)
                for g in range(4):
                    dve.wait_ge(grow_ps, 4 * n + g + 1)
                    dve.tensor_tensor(Am[q][:, 3 * g:3 * g + 3, :], pb[4 + g][:, 0:384].rearrange("p (c i) -> p c i", i=P),
                                      bc(SC[q][:, 0, g // 2, 3 * (g % 2):3 * (g % 2) + 3], P), ALU.subtract).then_inc(x_ready, 1)
                dve.wait_ge(x_ready, 4 * n + 4)
                dve.tensor_scalar(QKT[q][:, :, :], Am[q][:, :, :], 0.0, None, ALU.min).then_inc(xm_ready, 1)
                dve.wait_ge(xm_ready, 2 * n + 1)
                dve.tensor_scalar(Am[q][:, :, :], Am[q][:, :, :], 0.0, None, ALU.max).then_inc(xm_ready, 1)

            def decayed_q(n, q):
                dve.wait_ge(eg_ready, 4 * n + 4)
                for d in range(2):
                    dve.tensor_tensor(qd[q][:, NT * d:NT * d + 2, :], qd[q][:, NT * d:NT * d + 2, :], chunks(qS[q], 0, 2), ALU.mult)
                    ins = dve.tensor_tensor(qd[q][:, NT * d + 2:NT * d + 6, :], qd[q][:, NT * d + 2:NT * d + 6, :], chunks(qS[q], 2, 4), ALU.mult)
                ins.then_inc(qd_ready, 1)

            def with_decay(n, q):
                for buf, ps, b0, done in ((Am[q], kk_ps, 4, am_step), (QKT[q], qk_ps, 6, qkt_step)):
                    dve.wait_ge(ps, n + 1)
                    dve.wait_ge(dec_ready, 2 * n + 2)
                    for g in range(4):
                        x = buf[:, 3 * g:3 * g + 3, :].rearrange("p c i -> p (c i)")
                        dve.tensor_tensor(x, pb[b0 + g % 2][:, 0:384], x, ALU.mult).then_inc(done, 1)

            def beta_triangle(n, q):
                dve.wait_ge(am_step, 5 * n + 4)
                for m in range(NM):
                    ins = dve.scalar_tensor_tensor(Am[q][:, m, :], Am[q][:, m, :], SC[q][:, 4, m // NT, m % NT:m % NT + 1], STRICT[m // NT],
                                                   op0=ALU.mult, op1=ALU.mult)
                ins.then_inc(am_step, 1)

            PIECES = {1: (unit_length,), 2: (exponents,), 3: (decayed_q,), 4: (with_decay,), 5: (beta_triangle,)}

            def invert(n, q, prepare=True):
                for level in range(LEVELS):
                    for g in range(4):
                        dve.wait_ge(p_ps, 28 * n + 4 * level + g + 1)
                        dve.tensor_tensor(Pm[:, 3 * g:3 * g + 3, :], pb[g][:, 0:384].rearrange("p (c i) -> p c i", i=P),
                                          over(lvl[:, g // 2, level, :], 3), ALU.mult).then_inc(p_ready, 1)
                    if level == 0:
                        for g in range(4):
                            dve.wait_ge(p_ready, 28 * n + g + 1)
                            dve.tensor_tensor(TU[:, 1 + q, 3 * g:3 * g + 3, :], over(ident, 3), Pm[:, 3 * g:3 * g + 3, :], ALU.subtract).then_inc(tu_ready, 1)
                        continue
                    if prepare:
                        for piece in PIECES.get(level, ()):
                            piece(n + 1, 1 - q)
                    for g in range(4):
                        dve.wait_ge(x_ps, 24 * n + 4 * (level - 1) + g + 1)
                        if level < LEVELS - 1:
                            t = tu_ap(g, level, q)
                            src = pb[g][:, 0:384].rearrange("p (a b c) -> p a b c", a=2, c=1 << level)
                            dve.tensor_tensor(t, t, src, ALU.subtract).then_inc(tu_ready, 1)
                        else:
                            t = TU[:, 1 + q, 3 * g:3 * g + 3, :][:, :, 64 * (1 - g // 2):64 * (2 - g // 2)]
                            dve.tensor_tensor(t, t, pb[g][:, 192:384].rearrange("p (m c) -> p m c", m=3), ALU.subtract).then_inc(tu_ready, 1)

            def recur(n, q):
                for d in range(2):
                    dve.memset(St[d][:, :], 0.0).then_inc(s_new[d], 1)
                seen = {}
                for t in range(NT):
                    for d in range(2):
                        c = ORDER[d][t]
                        dve.wait_ge(ks_ps[d], NT * n + t + 1)
                        dve.scalar_tensor_tensor(rr[d][:, :], pb[4 * d][:, 0:P], SC[q][:, 1, d, c:c + 1], vN[q][:, c, :],
                                                 op0=ALU.mult, op1=ALU.add).then_inc(r_ready[d], 1)
                    for d in range(2):
                        c = ORDER[d][t]
                        dve.wait_ge(ds_ps[d], NT * n + t + 1)
                        dve.wait_ge(s_new[d], 7 * n + t + 1)
                        dve.scalar_tensor_tensor(St[d][:, :], St[d][:, :], SC[q][:, 3, d, c:c + 1], pb[4 * d + 3][:, 0:P],
                                                 op0=ALU.mult, op1=ALU.add).then_inc(s_new[d], 1)
                    for d in range(2):
                        c = ORDER[d][t]
                        dve.wait_ge(o_ps[d], NT * n + t + 1)
                        o = OB[:, c * P:(c + 1) * P]
                        if c in seen:
                            dve.wait_ge(o_sum[1 - d], NT * n + seen[c] + 1)
                            dve.tensor_tensor(o, pb[4 * d + 2][:, 0:P], o, ALU.add).then_inc(o_sum[d], 1)
                        else:
                            dve.tensor_copy(o, pb[4 * d + 2][:, 0:P]).then_inc(o_sum[d], 1)
                            seen[c] = t
                for d in range(2):
                    dve.wait_ge(o_sum[d], NT * n + NT)
                dve.tensor_scalar(qkv[:, ds(n), 0:TOK].rearrange("p a n -> p (a n)"), OB[:, 0:TOK], 1.0, None, ALU.mult).then_inc(head_out, 1)

            for level in range(1, 6):
                for piece in PIECES[level]:
                    piece(0, 0)
            dve.wait_ge(s_lvl, 16)

            def pair(i, last=False):
                invert(2 * i, 0)
                recur(2 * i, 0)
                invert(2 * i + 1, 1, prepare=not last)
                recur(2 * i + 1, 1)

            with dve.Fori(0, 3) as i:
                pair(i)
            pair(3, last=True)

            def y_low(h):
                dve.wait_ge(y_hi, h + 1)
                dve.tensor_tensor(hl[:, h, :], qkv[:, h, 0:TOK], hh[:, h, :], ALU.subtract).then_inc(y_lo, 1)

            split(S_DNOUT, 0, 0)
            dve.wait_ge(s_zin, 16)
            for h in range(HEADS):
                r = qkv[:, 8 + h, 0:TOK]
                dve.wait_ge(f_rc, h + 1)
                dve.scalar_tensor_tensor(r, qkv[:, h, 0:TOK], vecT[:, 2, 16:17], r, op0=ALU.mult, op1=ALU.mult).then_inc(f_y1, 1)
                dve.wait_ge(f_y1, h + 1)
                dve.tensor_tensor(qkv[:, h, 0:TOK], r, zin[:, h, :], ALU.mult).then_inc(f_y, 1)
                if h:
                    y_low(h - 1)
            y_low(HEADS - 1)

            def residual(s, o, u, layer, part, groups):
                dve.wait_ge(proj_done, s + 1)
                dve.wait_ge(drained, s)
                for i, (cols, n, v) in enumerate(groups):
                    x = xT[:, o, cols]
                    ins = dve.scalar_tensor_tensor(x, pb[2 * (u % 2) + i][:, 0:n], gate(layer, part, o, v), x, op0=ALU.mult, op1=ALU.add)
                ins.then_inc(drained, 1)

            for u in range(8):
                split_next(S_DNOUT + u, u % 4)
                residual(S_DNOUT + u, u, u, 0, 2, GROUPS)
            norm(1)

            def mlp(layer, blk, last=False):
                groups = norm_tokens[1 + 2 * layer]
                t0 = groups[-1][0].start
                base = (S_MLP0, S_MLP1)[layer]
                for u in range(16):
                    s = base + 16 * blk + u
                    if not (last and u == 15):
                        split_next(s, u % 4)
                    if u < 8:
                        m = 32 * layer + 8 * blk + u
                        dve.wait_ge(drained, s + 1)
                        if not (isinstance(m, int) and m < 2):
                            dve.wait_ge(hid_lo, m - 1)
                        dve.tensor_tensor(msq[:, u % 2, t0:TOK], mtmp[:, u % 2, t0:TOK], mtmp[:, u % 2, t0:TOK], ALU.mult).then_inc(sq_done, 1)
                        dve.wait_ge(sq_done, m + 1)
                        dve.wait_ge(hid_hi, m + 1)
                        dve.tensor_tensor(hidl[:, u, t0:TOK], msq[:, u % 2, t0:TOK], hidh[:, u, t0:TOK], ALU.subtract).then_inc(hid_lo, 1)
                    else:
                        residual(s, u - 8, u, layer, 5, groups)

            mlp(0, 0)
            with dve.Fori(1, 4) as blk:
                mlp(0, blk)
            take_mods(1, 0, 48, 7, 0, 96)
            take_wmod(2, 3)
            take_wmod(3, 3)
            norm(2)

            dve.wait_ge(s_rope, 32)
            dve.tensor_tensor(lamb[:, :, 0, :], lamb[:, :, 0, :], lamb[:, :, 1, :], ALU.mult).then_inc(lam_v, 1)
            dve.wait_ge(lam_v, 1)
            dve.tensor_reduce(sc32[:, 3, 0:2], lamb[:, :, 0, :], AX_X, ALU.add).then_inc(lam_v, 1)

            def qkvs(b, kind):
                for u in range(4):
                    s = S_QKV + 4 * b + u
                    split_next(s, u)
                    if kind == 2:
                        continue
                    o = 4 * b + u
                    r = row(qT, o) if kind == 0 else row(kT, o - 8)[:, LATS]
                    dve.wait_ge(drained, s + 1)
                    if o:
                        dve.wait_ge(rp_sin, o)
                    dve.tensor_tensor(rcs[:, :], r, ropt[:, 0, :], ALU.mult).then_inc(rp_cos, 1)
                    dve.tensor_tensor(rsw[:, u % 2, :], rsw[:, u % 2, :], ropt[:, 1, :], ALU.mult).then_inc(rp_sw, 1)
                    dve.wait_ge(rp_cos, o + 1)
                    dve.wait_ge(rp_sw, o + 1)
                    dve.tensor_tensor(r, rcs[:, :], rsw[:, u % 2, :], ALU.add).then_inc(rp_sin, 1)

            for b in range(6):
                qkvs(b, b // 2)
            dve.wait_ge(rp_sin, 16)
            dve.wait_ge(proj_done, S_DAOUT)
            for m in range(2):
                ins = dve.memset(qz[64 * (1 - m):64 * (2 - m), m, :], 0.0)
            ins.then_inc(qz_zero, 1)
            dve.wait_ge(lam_a, 1)
            dve.tensor_tensor(sc32[:, 3, 4:5], sc32[:, 3, 3:4], sc32[:, 3, 2:3], ALU.subtract).then_inc(lam_v, 1)
            dve.wait_ge(lam_v, 3)
            dve.tensor_scalar(sc32[:, 3, 5:6], sc32[:, 3, 4:5], -LAMBDA_INIT, None, ALU.add).then_inc(lam_v, 1)
            dve.tensor_scalar(sc32[:, 3, 6:7], vecT[:, 2, 17:18], 1.0 - LAMBDA_INIT, None, ALU.mult).then_inc(lam_v, 1)
            dve.wait_ge(lam_v, 5)

            def attend(h, first=False):
                for t in range(5):
                    if t < 4:
                        for m in range(2):
                            e = 8 * h + 2 * t + m
                            dve.wait_ge(s_ps, e + 1)
                            dve.tensor_reduce(ast[:, m, t:t + 1], sps[m][:, :, 0:384], mybir.AxisListType.XY, ALU.max).then_inc(mx_ready, 1)
                            dve.wait_ge(mx_ready, e + 1)
                            dve.tensor_scalar(ast[:, 2 + m, t:t + 1], ast[:, m, t:t + 1], -0.125, None, ALU.mult).then_inc(nm_ready, 1)
                    if t >= 1:
                        r, q = t - 1, (t - 1) % 2
                        dve.wait_ge(e_ready, 8 * h + 2 * r + 2)
                        dve.reciprocal(ast[:, 6:8, r:r + 1], ast[:, 4:6, r:r + 1]).then_inc(rl_ready, 1)
                        dve.wait_ge(rl_ready, 8 * h + 2 * r + 1)
                        dve.tensor_scalar(ast[:, 7, r:r + 1], ast[:, 7, r:r + 1], sc32[:, 3, 5:6], None, ALU.mult).then_inc(rl_ready, 1)
                        dve.tensor_scalar(pr[:, q, 0, :], pr[:, q, 0, :], ast[:, 6, r:r + 1], None, ALU.mult).then_inc(p0_ready, 1)
                        dve.wait_ge(rl_ready, 8 * h + 2 * r + 2)
                        dve.wait_ge(p0_ready, 4 * h + r + 1)
                        if not (first and r < 2):
                            dve.wait_ge(pt_ps, 4 * h + r - 1)
                        dve.scalar_tensor_tensor(pc[:, q, :], pr[:, q, 1, :], ast[:, 7, r:r + 1], pr[:, q, 0, :],
                                                 op0=ALU.mult, op1=ALU.add).then_inc(pc_ready, 1)
                        dve.wait_ge(pt_ps, 4 * h + r + 1)
                        if r == 0 and not first:
                            dve.wait_ge(at_ps, h)
                        for i in range(2):
                            ins = dve.tensor_copy(pT[:, 3 * i:3 * i + 3, r * P:(r + 1) * P], pb[i][:, 0:384].rearrange("p (c i) -> p c i", i=P))
                        ins.then_inc(pT_ready, 1)
                dve.wait_ge(a_rc, h + 1)
                dve.scalar_tensor_tensor(row(qT, h), osq[:, 1, :], sc32[:, 3, 6:7], orr[:, :], op0=ALU.mult, op1=ALU.mult).then_inc(a_y, 1)

            attend(0, first=True)
            with dve.Fori(1, HEADS) as h:
                attend(h)
            for h in range(HEADS):
                dve.wait_ge(y_hi, 8 + h + 1)
                dve.tensor_tensor(hl[:, h, LATS], qT[:, h, :], hh[:, h, LATS], ALU.subtract).then_inc(y_lo, 1)
            for u in range(8):
                split_next(S_DAOUT + u, u % 4)
                residual(S_DAOUT + u, u, u, 1, 2, GROUPS[:1])
            norm(3)
            mlp(1, 0)
            with dve.Fori(1, 3) as blk:
                mlp(1, blk)
            mlp(1, 3, last=True)
            norm(4)

        @block.tensor
        def _(pe):
            def matmul3(u, hi, lo, groups, s, chunk_ready=None, count=0):
                pe.wait_ge(lo_done, s + 1)
                if not (isinstance(s, int) and s < 2):
                    pe.wait_ge(drained, s - 1)
                for k in range(KC):
                    if chunk_ready is not None:
                        pe.wait_ge(chunk_ready, count + k + 1)
                    for j, (w, x) in enumerate(((whi, hi), (whi, lo), (wlo, hi))):
                        for i, (cols, n, v) in enumerate(groups):
                            ins = pe.matmul(pb[2 * (u % 2) + i][:, 0:n], w[u % 2][:, k, :], x[:, k, cols],
                                            start=(k == 0 and j == 0), stop=(k == KC - 1 and j == 2))
                ins.then_inc(proj_done, 1)

            def ada(a, par, nth, bank_, tile):
                pe.wait_ge(s_ada[par], nth)
                for k in range(KC):
                    ins = pe.matmul(pb[bank_][:, ds(2 * tile, 2)], adaw[par][:, k, :], cT[:, k, :], start=(k == 0), stop=(k == KC - 1))
                ins.then_inc(ada_done, 1)

            def norm(nu_):
                for k in range(KC):
                    pe.wait_ge(sq_ready, 8 * nu_ + k + 1)
                    for i, (cols, n, v) in enumerate(norm_tokens[nu_]):
                        ins = pe.matmul(pb[4 + i][:, 0:n], ones, sqb[:, k, cols], start=(k == 0), stop=(k == KC - 1))
                ins.then_inc(ss_ready, 1)

            pe.wait_ge(s_cst, 16)
            pe.wait_ge(s_vec, 144)
            pe.transpose(pb[7][:, 0:P], vecR[:, 0, :], ident)
            pe.transpose(pb[7][:, P:2 * P], vecR[:, 1, :], ident)
            pe.transpose(pb[7][:, 2 * P:2 * P + 18], vecR[0:18, 2, :], cst[0:18, 0, 0:18]).then_inc(vec_t, 1)
            pe.wait_ge(s_x, 32)
            for k in range(KC):
                if k >= 2:
                    pe.wait_ge(xT_lat, k - 1)
                    pe.wait_ge(xT_ctx, k - 1)
                for t in range(NT):
                    dst = pb[2 * (k % 2) + 1][:, t * P:(t + 1) * P] if t < 2 else pb[2 * (k % 2)][:, (t - 2) * P:(t - 1) * P]
                    ins = pe.transpose(dst, xin[:, t, k * P:(k + 1) * P], ident)
                ins.then_inc(xin_t, 1)
            pe.wait_ge(c_ready, 1)
            with pe.Fori(0, 8) as i:
                for j in range(2):
                    ada(2 * i + j, j, 16 * (i + 1), 6, 2 * i + j)
            norm(0)
            pe.wait_ge(hl_ready, 8)
            pe.wait_ge(wg_lo, 1)
            for t in range(NT):
                for k in range(KC):
                    for j, (x, w) in enumerate(((hh, wgh), (hl, wgh), (hh, wgl))):
                        ins = pe.matmul(pb[7][:, 32 * t:32 * (t + 1)], x[:, k, t * P:(t + 1) * P], w[:, k, :],
                                        start=(k == 0 and j == 0), stop=(k == KC - 1 and j == 2))
            ins.then_inc(gate_ps, 1)

            def dnin(b, first=False):
                for u in range(4):
                    s = 4 * b + u
                    matmul3(u, hh, hl, GROUPS, s)
                    if first and u == 0:
                        pe.wait_ge(gv, 6)
                        for d in range(2):
                            pe.matmul(pb[7][:, 48 * d:48 * (d + 1)], CUM[d], gdec[:, :, 8 * d:8 * d + 8], start=True, stop=True)
                        pe.matmul(pb[7][:, 96:192], ones, gdec[:, :, :], start=True, stop=True).then_inc(gp, 1)
                    ada(16 + s, u % 2, (s - u) * 8 + 16 * (u // 2 + 9), 6, 16 + s)

            dnin(0, first=True)
            with pe.Fori(1, 8) as b:
                dnin(b)

            def lengths(n, q):
                pe.wait_ge(l2_sq, n + 1)
                for i in range(4):
                    ins = pe.matmul(pb[4 + i][:, 0:386], ones, l2b[q][:, i // 2, (i % 2) * 386:(i % 2 + 1) * 386], start=True, stop=True)
                ins.then_inc(l2_ss, 1)

            def sums(n, q):
                pe.wait_ge(l2_sd, n + 1)
                for g in range(4):
                    pe.wait_ge(gu_ready, 2 * n + g // 2 + 1)
                    pe.matmul(pb[4 + g][:, 0:384], ones, QKT[q][:, 3 * g:3 * g + 3, :].rearrange("p c i -> p (c i)"), start=True, stop=True).then_inc(grow_ps, 1)

            def grams(n, q):
                pe.wait_ge(qk_ready, 2 * n + 2)
                pe.wait_ge(eg_ready, 4 * n + 4)
                for c in range(NT):
                    k = kS[q][:, off(c):off(c) + P]
                    ins = pe.matmul(pb[4 + c // 3][:, (c % 3) * P:(c % 3 + 1) * P], k, k, start=True, stop=True)
                ins.then_inc(kk_ps, 1)
                for c in range(NT):
                    ins = pe.matmul(pb[6 + c // 3][:, (c % 3) * P:(c % 3 + 1) * P], kS[q][:, off(c):off(c) + P], qS[q][:, off(c):off(c) + P], start=True, stop=True)
                ins.then_inc(qk_ps, 1)

            def token_major(n, q):
                pe.wait_ge(am_step, 5 * n + 4)
                pe.wait_ge(qkt_step, 4 * n + 4)
                for c in range(NT):
                    pe.transpose(pb[4 + c // 3][:, (c % 3) * P:(c % 3 + 1) * P], kS[q][:, off(c):off(c) + P], ident)
                for c in range(NT):
                    ins = pe.transpose(pb[6 + c // 3][:, (c % 3) * P:(c % 3 + 1) * P], vS[:, off(c):off(c) + P], ident)
                ins.then_inc(kv_t, 1)

            PIECES = {0: (lengths,), 1: (sums,), 3: (grams,), 5: (token_major,)}

            def invert(n, q, prepare=True):
                for level in range(LEVELS):
                    s = 1 << level
                    for g in range(4):
                        if level == 0:
                            pe.wait_ge(am_step, 5 * n + 5)
                        elif level:
                            pe.wait_ge(tu_ready, 28 * n + 4 * (level - 1) + g + 1)
                        for j in range(3):
                            m = 3 * g + j
                            if level:
                                ins = pe.matmul(pb[g][:, j * P:(j + 1) * P], Am[q][:, m, :], TU[:, 1 + q, m, :], start=True, stop=True)
                            else:
                                ins = pe.transpose(pb[g][:, j * P:(j + 1) * P], Am[q][:, m, :], ident)
                        ins.then_inc(p_ps, 1)
                    if level == 1:
                        pe.wait_ge(tu_init, n + 1)
                    for g in range(4 if level else 0):
                        pt, pu = ((0, 1), (1, 0))[g // 2]
                        pe.wait_ge(p_ready, 28 * n + 4 * level + g + 1)
                        for j in range(3):
                            m = 3 * g + j
                            if level < LEVELS - 1:
                                pe.matmul(pb[g][:, 64 * j:64 * (j + 1)].rearrange("p (b c) -> p b c", c=s), Pm[:, m, :],
                                          half(TU[:, 0, m, :], s, pt), start=True, stop=True)
                            ins = pe.matmul(pb[g][:, 192 + 64 * j:192 + 64 * (j + 1)].rearrange("p (b c) -> p b c", c=s), TU[:, 0, m, :],
                                            half(Pm[:, m, :], s, pu), start=True, stop=True)
                        ins.then_inc(x_ps, 1)
                    if prepare:
                        for piece in PIECES.get(level, ()):
                            piece(n + 1, 1 - q)

            def recur(n, q, ready=True):
                for t in range(NT):
                    if t == 0:
                        pe.wait_ge(ub_ready, 4 * n + 2)
                        pe.wait_ge(qkt_mask, n + 1)
                        pe.wait_ge(qd_ready, n + 1)
                        pe.wait_ge(kv_nat, n + (2 if ready else 1))
                        pe.wait_ge(tu_ready, 28 * n + 28)
                    elif t in (2, 3):
                        pe.wait_ge(ub_ready, 4 * n + t + 1)
                    for d in range(2):
                        c = ORDER[d][t]
                        pe.wait_ge(s_new[d], 7 * n + t + 1)
                        pe.matmul(pb[4 * d][:, 0:P], kS[q][:, off(c):off(c) + P], St[d][:, :], start=True, stop=True).then_inc(ks_ps[d], 1)
                        if t:
                            pe.wait_ge(o_sum[d], NT * n + t)
                        pe.matmul(pb[4 * d + 2][:, 0:P], St[d][:, :], qd[q][:, NT * d + c, :], start=True, stop=False)
                    for d in range(2):
                        c = ORDER[d][t]
                        pe.wait_ge(r_ready[d], NT * n + t + 1)
                        pe.matmul(pb[4 * d + 1][:, 0:P], TU[:, 1 + q, NT * d + c, :], rr[d][:, :], start=True, stop=True).then_inc(nu_ps[d], 1)
                    for d in range(2):
                        c = ORDER[d][t]
                        pe.wait_ge(nu_ready[d], 2 * (NT * n + t) + 1)
                        pe.matmul(pb[4 * d + 3][:, 0:P], kN[q][:, c, :], nuk[d][:, :], start=True, stop=True).then_inc(ds_ps[d], 1)
                    for d in range(2):
                        c = ORDER[d][t]
                        pe.wait_ge(nu_ready[d], 2 * (NT * n + t) + 2)
                        pe.matmul(pb[4 * d + 2][:, 0:P], nu[d][:, :], QKT[q][:, NT * d + c, :], start=False, stop=True).then_inc(o_ps[d], 1)
                for d in range(2):
                    pe.wait_ge(o_sum[d], NT * n + NT)

            pe.wait_ge(drained, S_DNOUT)
            pe.wait_ge(mod_ready, 2)
            for level in (0, 1, 3, 5):
                for piece in PIECES[level]:
                    piece(0, 0)

            def pair(i, last=False):
                invert(2 * i, 0)
                recur(2 * i, 0)
                invert(2 * i + 1, 1, prepare=not last)
                recur(2 * i + 1, 1, ready=not last)

            with pe.Fori(0, 3) as i:
                pair(i)
            pair(3, last=True)
            for h in range(HEADS):
                pe.wait_ge(f_sq, h + 1)
                if h >= 4:
                    pe.wait_ge(f_sd, h - 3)
                for i in range(2):
                    ins = pe.matmul(pb[2 * (h % 4) + i][:, 0:384], ones, qkv[:, 8 + h, 384 * i:384 * (i + 1)], start=True, stop=True)
                ins.then_inc(f_ss, 1)
            for u in range(8):
                matmul3(u, hh, hl, GROUPS, S_DNOUT + u, None if u else y_lo, 0)
            norm(1)

            def mlp(layer, blk):
                groups = norm_tokens[1 + 2 * layer]
                base = (S_MLP0, S_MLP1)[layer]
                for u in range(16):
                    s = base + 16 * blk + u
                    if u == 0:
                        matmul3(u, hh, hl, groups, s, hl_ready, 8 + 16 * layer)
                    elif u < 8:
                        matmul3(u, hh, hl, groups, s)
                    elif u == 8:
                        matmul3(u, hidh, hidl, groups, s, hid_lo, 32 * layer + 8 * blk)
                    else:
                        matmul3(u, hidh, hidl, groups, s)
                    if layer == 0 and u < 12:
                        tile = 12 * blk + u
                        ada(48 + tile, u % 2, 96 * blk + 16 * (25 + u // 2), 7, tile)

            with pe.Fori(0, 4) as blk:
                mlp(0, blk)
            norm(2)
            for b in range(6):
                for u in range(4):
                    matmul3(u, hh, hl, GROUPS[:1] if b < 2 else GROUPS, S_QKV + 4 * b + u, hl_ready if b + u == 0 else None, 16)

            def attend(h, first=False):
                pe.wait_ge(qz_ready, h + 1)
                if first:
                    pe.wait_ge(drained, S_DAOUT)
                else:
                    pe.wait_ge(pT_ready, 4 * h)
                for c in range(NT):
                    ins = pe.transpose(pb[c // 3][:, (c % 3) * P:(c % 3 + 1) * P], vs2[:, c * P:(c + 1) * P], ident)
                ins.then_inc(vt_ps, 1)

                def scores(t):
                    for m in range(2):
                        if not (first and t == 0):
                            pe.wait_ge(e_ready, 8 * h + 2 * t + m - 1)
                        for i in range(2):
                            ins = pe.matmul(sps[m][:, i, 0:384], qz[:, m, t * P:(t + 1) * P], row(kT, h)[:, 384 * i:384 * (i + 1)], start=True, stop=True)
                        ins.then_inc(s_ps, 1)

                scores(0)
                for t in range(4):
                    if t < 3:
                        scores(t + 1)
                    pe.wait_ge(pc_ready, 4 * h + t + 1)
                    if t == 0:
                        pe.wait_ge(vn_ready, h + 1)
                    else:
                        pe.wait_ge(pT_ready, 4 * h + t)
                    for c in range(NT):
                        ins = pe.transpose(pb[c // 3][:, (c % 3) * P:(c % 3 + 1) * P], pc[:, t % 2, c * P:(c + 1) * P], ident)
                    ins.then_inc(pt_ps, 1)
                pe.wait_ge(pT_ready, 4 * h + 4)
                for c in range(NT):
                    ins = pe.matmul(pb[6][:, :], vn[:, c, :], pT[:, c, :], start=(c == 0), stop=(c == NT - 1))
                ins.then_inc(at_ps, 1)
                pe.wait_ge(a_sq, h + 1)
                pe.matmul(pb[7][:, :], ones, osq[:, 0, :], start=True, stop=True).then_inc(a_ss, 1)

            attend(0, first=True)
            with pe.Fori(1, HEADS) as h:
                attend(h)
            for u in range(8):
                matmul3(u, hh, hl, GROUPS[:1], S_DAOUT + u, None if u else y_lo, 8)
            norm(3)
            with pe.Fori(0, 4) as blk:
                mlp(1, blk)
            norm(4)
            pe.wait_ge(fin_n, 8)
            for t in range(4):
                for i in range(2):
                    j = 2 * t + i
                    if j >= 4:
                        pe.wait_ge(fin_ready, j - 3)
                    for k in range(4):
                        ins = pe.transpose(pb[j % 4][:, k * P:(k + 1) * P], sqb[:, 4 * i + k, CTX + t * P:CTX + (t + 1) * P], ident)
                    ins.then_inc(fin_ps, 1)


_INS = ["x", "c", "ctx", "c_ctx", "ada_w", "ada_b", "norm_w", "mlp_w1", "mlp_w2", "dn_w_in", "dn_conv", "dn_a_log",
        "dn_dt_bias", "dn_out_norm", "dn_w_out", "da_w_qkv", "da_lambda", "da_subln", "da_w_out", "final_norm"]


def kernel(**inputs):
    import concourse.bacc as _bacc
    from concourse.bass_utils import run_bass_kernel_spmd as _run

    nc = _bacc.Bacc("TRN2", target_bir_lowering=False, num_devices=1)
    arrays, args = {}, {}
    cst, lvl, rope = constants()
    for name, a in [(n, np.ascontiguousarray(inputs[n])) for n in _INS] + [("cst", cst), ("lvl", lvl), ("rope", rope)]:
        arrays[f"in_{name}"] = a
        args[name] = nc.dram_tensor(f"in_{name}", a.shape, mybir.dt.from_np(a.dtype), kind="ExternalInput").ap()
    args["out"] = nc.dram_tensor("out_0", (1, LAT, D), F32, kind="ExternalOutput").ap()
    build(nc, args)
    r = _run(nc, [arrays], core_ids=[0])
    return r.results[0]["out_0"]
```
